# Optimizing a Trainium2 kernel written in Bass

```python
import jax, jax.numpy as jnp
from jax import lax
import numpy as np

D_MODEL = 2048
BATCH = 1
SEQ = 256
DEPTH = 1

D_MIX = D_MODEL
ATTN_HEADS = 8
HEAD_DIM = 128
D_ATTN = ATTN_HEADS * HEAD_DIM
SGU_GROUPS = 8
SGU_GROUP_DIM = (D_MIX - D_ATTN) // SGU_GROUPS
D_SGU = SGU_GROUPS * SGU_GROUP_DIM
D_IN = 3 * D_ATTN + 2 * D_SGU
MOBA_BLOCK = 256
MOBA_TOPK = 3
Q_CHUNK = 32
SGU_CHUNK = 128
D_FF = 5632
EPS = 1e-6
NEG_INF = -1e30

kernel_name = 'hymba_moba_sgu_macaron'

def rmsnorm(x, g):
    xf = x.astype(jnp.float32)
    y = xf * lax.rsqrt(jnp.mean(xf * xf, axis=-1, keepdims=True) + EPS)
    return (y * g.astype(jnp.float32)).astype(x.dtype)

def swiglu(h, w_gate, w_up, w_down):
    return (jax.nn.silu(h @ w_gate) * (h @ w_up)) @ w_down

def pad_seq(a, axis, multiple):
    s = a.shape[axis]
    s_pad = -(-s // multiple) * multiple
    widths = [(0, 0)] * a.ndim
    widths[axis] = (0, s_pad - s)
    return jnp.pad(a, widths), s_pad

def moba_attention(q, k, v):
    B, H, S, Dh = q.shape
    q, S_pad = pad_seq(q, 2, MOBA_BLOCK)
    k, _ = pad_seq(k, 2, MOBA_BLOCK)
    v, _ = pad_seq(v, 2, MOBA_BLOCK)
    nb = S_pad // MOBA_BLOCK
    kb = k.reshape(B, H, nb, MOBA_BLOCK, Dh)
    vb = v.reshape(B, H, nb, MOBA_BLOCK, Dh)
    k_mean = jnp.mean(kb.astype(jnp.float32), axis=3)
    q_blk = jnp.arange(S_pad) // MOBA_BLOCK
    gate = jnp.einsum('bhsd,bhnd->bhsn', q.astype(jnp.float32), k_mean)
    fully_past = jnp.arange(nb)[None, :] < q_blk[:, None]
    gate = jnp.where(fully_past, gate, NEG_INF)
    topk = min(MOBA_TOPK, nb)
    _, sel_idx = lax.top_k(gate, topk)
    sel_valid = jnp.arange(topk)[None, :] < q_blk[:, None]
    gather = jax.vmap(jax.vmap(lambda blocks, ids: blocks[ids]))
    scale = HEAD_DIM ** -0.5

    def chunk(c):
        start = c * Q_CHUNK
        q_c = lax.dynamic_slice_in_dim(q, start, Q_CHUNK, axis=2)
        idx_c = lax.dynamic_slice_in_dim(sel_idx, start, Q_CHUNK, axis=2)
        valid_c = lax.dynamic_slice_in_dim(sel_valid, start, Q_CHUNK, axis=0)
        own = start // MOBA_BLOCK
        k_own = lax.dynamic_index_in_dim(kb, own, axis=2, keepdims=False)
        v_own = lax.dynamic_index_in_dim(vb, own, axis=2, keepdims=False)
        q_pos = start + jnp.arange(Q_CHUNK)
        k_pos = own * MOBA_BLOCK + jnp.arange(MOBA_BLOCK)
        s_own = jnp.einsum('bhqd,bhkd->bhqk', q_c, k_own).astype(jnp.float32) * scale
        s_own = jnp.where(k_pos[None, :] <= q_pos[:, None], s_own, NEG_INF)
        k_sel = gather(kb, idx_c)
        v_sel = gather(vb, idx_c)
        s_sel = jnp.einsum('bhqd,bhqjkd->bhqjk', q_c, k_sel).astype(jnp.float32) * scale
        s_sel = jnp.where(valid_c[:, :, None], s_sel, NEG_INF)
        s_all = jnp.concatenate(
            [s_own, s_sel.reshape(B, H, Q_CHUNK, topk * MOBA_BLOCK)], axis=-1)
        p = jax.nn.softmax(s_all, axis=-1).astype(v.dtype)
        p_own = p[..., :MOBA_BLOCK]
        p_sel = p[..., MOBA_BLOCK:].reshape(B, H, Q_CHUNK, topk, MOBA_BLOCK)
        return (jnp.einsum('bhqk,bhkd->bhqd', p_own, v_own)
                + jnp.einsum('bhqjk,bhqjkd->bhqd', p_sel, v_sel))

    out = lax.map(chunk, jnp.arange(S_pad // Q_CHUNK))
    out = out.transpose(1, 2, 0, 3, 4).reshape(B, H, S_pad, Dh)
    return out[:, :, :S]

def spatial_gating(z, ln_g, ln_b, w_s, b_s):
    B, S, _ = z.shape
    u, g = jnp.split(z, 2, axis=-1)
    g = g.reshape(B, S, SGU_GROUPS, SGU_GROUP_DIM)
    gf = g.astype(jnp.float32)
    mu = jnp.mean(gf, axis=-1, keepdims=True)
    var = jnp.mean(jnp.square(gf - mu), axis=-1, keepdims=True)
    gf = (gf - mu) * lax.rsqrt(var + EPS)
    g = (gf * ln_g.reshape(SGU_GROUPS, SGU_GROUP_DIM)
         + ln_b.reshape(SGU_GROUPS, SGU_GROUP_DIM)).astype(z.dtype)
    g, S_pad = pad_seq(g, 1, SGU_CHUNK)
    gc = g.reshape(B, S_pad // SGU_CHUNK, SGU_CHUNK, SGU_GROUPS, SGU_GROUP_DIM)
    w = jnp.tril(w_s)
    mixed = jnp.einsum('gts,bnsgc->bntgc', w, gc) + b_s.T[None, None, :, :, None]
    mixed = mixed.reshape(B, S_pad, D_SGU)[:, :S]
    return u * mixed

def setup_inputs(seed: int = 0) -> dict:
    key = jax.random.key(seed)
    ks = jax.random.split(key, 20)
    n = lambda k, shape, s: jax.random.normal(k, shape, jnp.float32) * s
    gain = lambda k, shape: 1.0 + 0.05 * jax.random.normal(k, shape, jnp.float32)
    L = DEPTH
    return {
        'x': n(ks[0], (BATCH, SEQ, D_MODEL), 1.0),
        'ffn1_norm': gain(ks[1], (L, D_MODEL)),
        'ffn1_w_gate': n(ks[2], (L, D_MODEL, D_FF), D_MODEL ** -0.5),
        'ffn1_w_up': n(ks[3], (L, D_MODEL, D_FF), D_MODEL ** -0.5),
        'ffn1_w_down': n(ks[4], (L, D_FF, D_MODEL), D_FF ** -0.5),
        'mix_norm': gain(ks[5], (L, D_MODEL)),
        'w_in': n(ks[6], (L, D_MODEL, D_IN), D_MODEL ** -0.5),
        'q_norm': gain(ks[7], (L, HEAD_DIM)),
        'k_norm': gain(ks[8], (L, HEAD_DIM)),
        'sgu_ln_gain': gain(ks[9], (L, D_SGU)),
        'sgu_ln_bias': n(ks[10], (L, D_SGU), 0.02),
        'sgu_w_spatial': n(ks[11], (L, SGU_GROUPS, SGU_CHUNK, SGU_CHUNK), 0.5 * SGU_CHUNK ** -0.5),
        'sgu_b_spatial': 1.0 + 0.1 * jax.random.normal(ks[12], (L, SGU_GROUPS, SGU_CHUNK), jnp.float32),
        'attn_out_gain': gain(ks[13], (L, D_ATTN)),
        'sgu_out_gain': gain(ks[14], (L, D_SGU)),
        'w_out': n(ks[15], (L, D_MIX, D_MODEL), D_MIX ** -0.5),
        'ffn2_norm': gain(ks[16], (L, D_MODEL)),
        'ffn2_w_gate': n(ks[17], (L, D_MODEL, D_FF), D_MODEL ** -0.5),
        'ffn2_w_up': n(ks[18], (L, D_MODEL, D_FF), D_MODEL ** -0.5),
        'ffn2_w_down': n(ks[19], (L, D_FF, D_MODEL), D_FF ** -0.5),
    }

def reference(x, ffn1_norm, ffn1_w_gate, ffn1_w_up, ffn1_w_down, mix_norm, w_in,
              q_norm, k_norm, sgu_ln_gain, sgu_ln_bias, sgu_w_spatial, sgu_b_spatial,
              attn_out_gain, sgu_out_gain, w_out, ffn2_norm, ffn2_w_gate, ffn2_w_up,
              ffn2_w_down):
    B, S, _ = x.shape
    for l in range(DEPTH):
        h = rmsnorm(x, ffn1_norm[l])
        x = x + 0.5 * swiglu(h, ffn1_w_gate[l], ffn1_w_up[l], ffn1_w_down[l])
        h = rmsnorm(x, mix_norm[l])
        proj = h @ w_in[l]
        q = proj[..., :D_ATTN]
        k = proj[..., D_ATTN:2 * D_ATTN]
        v = proj[..., 2 * D_ATTN:3 * D_ATTN]
        z = proj[..., 3 * D_ATTN:]
        to_heads = lambda t: t.reshape(B, S, ATTN_HEADS, HEAD_DIM).transpose(0, 2, 1, 3)
        q = rmsnorm(to_heads(q), q_norm[l])
        k = rmsnorm(to_heads(k), k_norm[l])
        v = to_heads(v)
        attn = moba_attention(q, k, v).transpose(0, 2, 1, 3).reshape(B, S, D_ATTN)
        sgu = spatial_gating(jax.nn.gelu(z), sgu_ln_gain[l], sgu_ln_bias[l],
                             sgu_w_spatial[l], sgu_b_spatial[l])
        mixed = jnp.concatenate(
            [rmsnorm(attn, attn_out_gain[l]), rmsnorm(sgu, sgu_out_gain[l])], axis=-1)
        x = x + mixed @ w_out[l]
        h = rmsnorm(x, ffn2_norm[l])
        x = x + 0.5 * swiglu(h, ffn2_w_gate[l], ffn2_w_up[l], ffn2_w_down[l])
    return x


_drawn_inputs = setup_inputs


def setup_inputs(seed=0):
    import zlib

    import numpy as np

    out = dict(_drawn_inputs(seed))
    spreads = {}
    factors = {'sgu_ln_gain': 7.062, 'sgu_ln_bias': 34.419, 'ffn2_norm': 3.972}
    for name, (base, spread) in spreads.items():
        noise = np.random.default_rng([zlib.crc32(name.encode()), seed]).standard_normal(out[name].shape)
        drawn = base * np.exp(spread * noise) if base else spread * noise
        out[name] = __import__('jax').numpy.asarray(drawn.astype(out[name].dtype))
    for name, factor in factors.items():
        out[name] = (out[name] * factor).astype(out[name].dtype)
    return out
```

```python
from contextlib import ExitStack

import concourse.bass as bass
from concourse import mybir

ALU = mybir.AluOpType
ACT = mybir.ActivationFunctionType
AXX = mybir.AxisListType.X
F32 = mybir.dt.float32
F32R = mybir.dt.float32r

P = 128
NCOL = 512
TOK = 2
D = 2048
DFF = 5632
HEADS = 8
HD = 128
DATT = HEADS * HD
SGU_G = 8
KT = D // P
FT = DFF // P
CHUNKS = DFF // NCOL
XG = D // NCOL
PG = (3 * DATT + 2 * DATT) // NCOL
RAW = 4
SPL = 4
EPS = 1e-6
SCALE = float(HD) ** -0.5
NEG = -1e30

HALVES_D = [(2 * j, 2) for j in range(KT // 2)]
HALVES_F = [(11 * (j // 6) + 2 * (j % 6), 1 if j % 6 == 5 else 2) for j in range(24)]
assert sum(n for _, n in HALVES_F) == FT and D % P == 0
ND, NF = len(HALVES_D), len(HALVES_F)

GU0 = [0, 0]
DN0 = [0, 0]
GU0[0] = 0
DN0[0] = GU0[0] + CHUNKS * 2 * ND
IN0 = DN0[0] + XG * NF
OUT0 = IN0 + PG * ND
GU0[1] = OUT0 + XG * ND
DN0[1] = GU0[1] + CHUNKS * 2 * ND
assert all(h % (2 * RAW) == 0 for h in GU0 + DN0 + [IN0, OUT0])

TX0 = 0
TA = [TX0 + 2 * XG, 0]
TY1 = TA[0] + 2 * CHUNKS
TWS = TY1 + 2 * XG
TQK = TWS + 2
TP = TQK + 8
TAT = TP + HEADS
TSG = TAT + 4
TY2 = TSG + 4
TA[1] = TY2 + 2 * XG
SX0 = 0
SA = [SX0 + 2 * XG, 0]
SY1 = SA[0] + 2 * CHUNKS
SAT = SY1 + 2 * XG
SSG = SAT + 4
SY2 = SSG + 4
SA[1] = SY2 + 2 * XG

ROOTS = ["ffn1", "mix", "qk0", "qk1", "qk2", "qk3", "ln0", "attn", "ln1", "sgu", "ffn2"]

V_FFN1, V_MIX, V_FFN2, V_ATT, V_SGU, V_Q, V_K, V_BS = 0, 16, 32, 48, 56, 64, 65, 66
NVEC = 74


def build(nc, x, ffn1_norm, ffn1_w_gate, ffn1_w_up, ffn1_w_down, mix_norm, w_in, q_norm, k_norm,
          sgu_ln_gain, sgu_ln_bias, sgu_w_spatial, sgu_b_spatial, attn_out_gain, sgu_out_gain, w_out,
          ffn2_norm, ffn2_w_gate, ffn2_w_up, ffn2_w_down, out):
    w_gate = [ffn1_w_gate[0], ffn2_w_gate[0]]
    w_up = [ffn1_w_up[0], ffn2_w_up[0]]
    w_down = [ffn1_w_down[0], ffn2_w_down[0]]
    x_rows = x[0].rearrange("(t p) d -> p t d", p=P)
    out_rows = out[0].rearrange("(t p) d -> p t d", p=P)

    with ExitStack() as ctx:
        def sb(name, shape, dt=F32, where=ctx):
            return where.enter_context(nc.sbuf_tensor(name, shape, dt))

        def sem(name):
            return ctx.enter_context(nc.semaphore(name))

        x_sb = sb("x_sb", [P, TOK, D])
        xt_hi = sb("xt_hi", [P, KT, TOK * P], F32R)
        xt_lo = sb("xt_lo", [P, KT, TOK * P], F32R)
        raw = sb("raw", [P, RAW, 4 * NCOL])
        w_hi = sb("w_hi", [P, SPL, 2 * NCOL], F32R)
        w_lo = sb("w_lo", [P, SPL, 2 * NCOL], F32R)
        stage = sb("stage", [P, TOK, NCOL])
        ident = sb("ident", [P, P])
        vec = sb("vec", [P, NVEC])
        stats = sb("stats", [P, TOK, XG, 6])
        agg = sb("agg", [P, TOK, 2])
        mean_sq = sb("mean_sq", [P, len(ROOTS), 8])
        root = sb("root", [P, len(ROOTS), 8])
        neg_half = sb("neg_half", [P, 8])

        with ExitStack() as ffn:
            at1_hi = sb("at1_hi", [P, FT, TOK * P], F32R, ffn)
            at1_lo = sb("at1_lo", [P, FT, TOK * P], F32R, ffn)
        with ExitStack() as mixer:
            q_sb = sb("q_sb", [P, TOK, DATT], F32, mixer)
            k_sb = sb("k_sb", [P, TOK, DATT], F32, mixer)
            v_sb = sb("v_sb", [P, TOK, DATT], F32, mixer)
            qt = sb("qt", [P, HEADS, TOK * P], F32, mixer)
            kt = sb("kt", [P, HEADS, TOK * P], F32, mixer)
            mt_hi = sb("mt_hi", [P, KT, TOK * P], F32R, mixer)
            mt_lo = sb("mt_lo", [P, KT, TOK * P], F32R, mixer)
            wst = sb("wst", [P, SGU_G, P], F32, mixer)
            s_sb = sb("s_sb", [P, 2, 3 * P], F32, mixer)
            pt = sb("pt", [P, 2, 3 * P], F32, mixer)
            mask = sb("mask", [P, 3 * P], F32, mixer)
            sq_sum = sb("sq_sum", [P, TOK, 4], F32, mixer)
            neg_max = sb("neg_max", [P, HEADS, TOK], F32, mixer)
            row_sum = sb("row_sum", [P, HEADS, TOK], F32, mixer)
            inv_sum = sb("inv_sum", [P, HEADS, TOK], F32, mixer)
            ln_stats = sb("ln_stats", [P, TOK, 4, 6], F32, mixer)
            ln_agg = sb("ln_agg", [P, TOK, 4, 2], F32, mixer)
        with ExitStack() as ffn:
            at2_hi = sb("at2_hi", [P, FT, TOK * P], F32R, ffn)
            at2_lo = sb("at2_lo", [P, FT, TOK * P], F32R, ffn)
        at_hi, at_lo = [at1_hi, at2_hi], [at1_lo, at2_lo]
        vec_rows = stage[0:NVEC, 0, 0:P]
        ws_raw = kt[:, 0:4, :].rearrange("p a (b s) -> p (a b) s", s=P)
        ln_rows = kt[:, :, :].rearrange("p h t -> p (h t)").rearrange("p (a c) -> p a c", a=2)

        gate_ps = ctx.enter_context(nc.psum_tensor("gate_ps", [P, TOK, NCOL], F32))
        up_ps = ctx.enter_context(nc.psum_tensor("up_ps", [P, TOK, NCOL], F32))
        y_ps = ctx.enter_context(nc.psum_tensor("y_ps", [P, TOK, NCOL], F32))
        turn_ps = ctx.enter_context(nc.psum_tensor("turn_ps", [P, 2, NCOL], F32))

        raw_landed = [sem(f"raw_landed{s}") for s in range(RAW)]
        hi_ready = sem("hi_ready")
        lo_ready = sem("lo_ready")
        split_used = sem("split_used")
        gate_done, gate_taken = sem("gate_done"), sem("gate_taken")
        up_done, gated_ready = sem("up_done"), sem("gated_ready")
        y_done, x_ready = sem("y_done"), sem("x_ready")
        x_saved = sem("x_saved")
        turn_full = sem("turn_full")
        turn_high = sem("turn_high")
        turned = sem("turned")
        vec_landed, x_landed = sem("vec_landed"), [sem(f"x_landed{g}") for g in range(XG)]
        ident_ready, vec_turned, vec_ready = sem("ident_ready"), sem("vec_turned"), sem("vec_ready")
        pool_step, dve_step = sem("pool_step"), sem("dve_step")
        ms_ready, root_ready = sem("ms_ready"), sem("root_ready")
        proj_done, proj_taken = sem("proj_done"), sem("proj_taken")
        qk_scaled = sem("qk_scaled")
        ws_landed, ws_masked, mask_ready = sem("ws_landed"), sem("ws_masked"), sem("mask_ready")
        ln_landed, ln_ready = sem("ln_landed"), sem("ln_ready")
        s_done, max_ready, p_ready = sem("s_done"), sem("max_ready"), sem("p_ready")
        o_done, o_taken = sem("o_done"), sem("o_taken")
        attn_scaled, sgu_scaled = sem("attn_scaled"), sem("sgu_scaled")
        mixed_done, mixed_taken = sem("mixed_done"), sem("mixed_taken")
        gated_u = sem("gated_u")
        out_landed = [sem(f"out_landed{t}") for t in range(TOK)]

        def sum_done(eng, done, group, last_half, t):
            if t == 0:
                eng.wait_ge(done, group + 1)
            else:
                eng.wait_ge(split_used, last_half + 1)

        psum_of = [gate_ps, up_ps]
        rows_of = {"ffn1": V_FFN1, "mix": V_MIX, "ffn2": V_FFN2}
        block = ctx.enter_context(nc.Block())

        @block.sync
        def _(sp):
            def load(weights, col, halves, piece, j, first=False):
                k0 = halves[2 * j][0]
                n = halves[2 * j][1] + halves[2 * j + 1][1]
                if not first:
                    sp.wait_ge(lo_ready, 2 * piece - 2 * RAW + 2)
                src = weights[k0 * P:(k0 + n) * P, col].rearrange("(k p) n -> p k n", p=P)
                dst = raw[:, j % RAW, 0:n * NCOL].rearrange("p (k n) -> p k n", n=NCOL)
                sp.dma_start(dst, src).then_inc(raw_landed[j % RAW], 16)

            def gate_up(f, c, first=False):
                piece = GU0[f] // 2 + c * ND
                for j in range(ND // 2):
                    load(w_gate[f], bass.ts(c, NCOL), HALVES_D, piece + j, j, first)
                for j in range(ND // 2):
                    load(w_up[f], bass.ts(c, NCOL), HALVES_D, piece + ND // 2 + j, j)

            def groups(weights, halves, start, n, shift=0):
                with sp.Fori(0, n) as g:
                    for j in range(len(halves) // 2):
                        load(weights, bass.ts(g + shift, NCOL), halves, start // 2 + g * (len(halves) // 2) + j, j)

            gate_up(0, 0, first=True)
            with sp.Fori(1, CHUNKS) as c:
                gate_up(0, c)
            groups(w_down[0], HALVES_F, DN0[0], XG)
            groups(w_in[0], HALVES_D, IN0, 6)
            groups(w_in[0], HALVES_D, IN0 + 6 * ND, 2, shift=8)
            groups(w_in[0], HALVES_D, IN0 + 8 * ND, 2, shift=6)
            groups(w_out[0], HALVES_D, OUT0, XG)
            with sp.Fori(0, CHUNKS) as c:
                gate_up(1, c)
            groups(w_down[1], HALVES_F, DN0[1], XG)

        @block.tensor
        def _(pe):
            def half(n, j, k0, kn, lhs_hi, lhs_lo, dst, last_k, done, free=None):
                pe.wait_ge(lo_ready, n + 1)
                for t in range(TOK):
                    if free is not None:
                        pe.wait_ge(free[0], free[1] + t + 1)
                    for k in range(k0, k0 + kn):
                        hi = w_hi[:, j % SPL, (k - k0) * NCOL:(k - k0 + 1) * NCOL]
                        lo = w_lo[:, j % SPL, (k - k0) * NCOL:(k - k0 + 1) * NCOL]
                        a_hi = lhs_hi[:, k, t * P:(t + 1) * P]
                        a_lo = lhs_lo[:, k, t * P:(t + 1) * P]
                        pe.matmul(dst[:, t, :], a_hi, hi, start=(k == 0), stop=False)
                        pe.matmul(dst[:, t, :], a_hi, lo, start=False, stop=False)
                        mm = pe.matmul(dst[:, t, :], a_lo, hi, start=False, stop=(k == last_k))
                    if k == last_k and t == 0:
                        mm.then_inc(done, 1)
                mm.then_inc(split_used, 1)

            def turn_stage(u, ready, value):
                pe.wait_ge(ready, value)
                for b in range(2):
                    pe.wait_ge(turned, u + b - 1)
                    for kk in range(2):
                        for t in range(TOK):
                            mm = pe.transpose(turn_ps[:, b, kk * 256 + t * P:kk * 256 + (t + 1) * P],
                                              stage[:, t, (2 * b + kk) * P:(2 * b + kk + 1) * P], ident[:, :])
                    mm.then_inc(turn_full, 1)

            def gate_up(f, c, job, free=True, need=None):
                n = GU0[f] + c * 2 * ND
                for j, (k0, kn) in enumerate(HALVES_D):
                    if need and k0 in need:
                        pe.wait_ge(turned, need[k0])
                    half(n + j, j, k0, kn, xt_hi, xt_lo, gate_ps, KT - 1, gate_done,
                         (gate_taken, 2 * (CHUNKS * f + c - 1)) if free and j == 0 else None)
                    if j == 1:
                        job()
                for j, (k0, kn) in enumerate(HALVES_D):
                    half(n + ND + j, j, k0, kn, xt_hi, xt_lo, up_ps, KT - 1, up_done,
                         (gated_ready, 2 * (CHUNKS * f + c - 1)) if free and j == 0 else None)

            def turn_gated(f, c):
                turn_stage(TA[f] + 2 * c, gated_ready, 2 * (CHUNKS * f + c) + 2)

            def down(f, g, job, first=False):
                n = DN0[f] + g * NF
                for j, (k0, kn) in enumerate(HALVES_F):
                    if first and k0 + kn > FT - 4:
                        pe.wait_ge(turned, TA[f] + 2 * CHUNKS)
                    half(n + j, j, k0, kn, at_hi[f], at_lo[f], y_ps, FT - 1, y_done,
                         (x_ready, 2 * (2 * XG * f + g - 1)) if j == 0 and not first else None)
                    if j == 1:
                        job()

            def ffn(f):
                if f:
                    gate_up(f, 0, lambda: turn_stage(TY2 + 2 * (XG - 1), x_ready, 4 * XG), free=False,
                            need={0: TY2 + 2 * (XG - 1), (XG - 1) * 4: TY2 + 2 * XG})
                else:
                    gate_up(f, 0, lambda: None, free=False, need={k: TX0 + k // 2 + 2 for k in range(0, KT, 4)})
                with pe.Fori(1, CHUNKS) as c:
                    gate_up(f, c, lambda: turn_gated(f, c - 1))
                down(f, 0, lambda: turn_gated(f, CHUNKS - 1), first=True)
                with pe.Fori(1, XG) as g:
                    down(f, g, (lambda: None) if f else
                         (lambda: turn_stage(TY1 + 2 * (g - 1), x_ready, 2 * (2 * XG * f + g - 1) + 2)))

            pe.wait_ge(ident_ready, 2)
            pe.wait_ge(vec_landed, 16 * 8)
            pe.transpose(y_ps[:, 0, 0:NVEC], vec_rows, ident[0:NVEC, 0:NVEC]).then_inc(vec_turned, 1)
            for g in range(XG):
                pe.wait_ge(x_landed[g], 16)
                for b in range(2):
                    u = TX0 + 2 * g + b
                    if u >= 2:
                        pe.wait_ge(turned, u - 1)
                    for kk in range(2):
                        k = 4 * g + 2 * b + kk
                        for t in range(TOK):
                            mm = pe.transpose(turn_ps[:, b, kk * 256 + t * P:kk * 256 + (t + 1) * P],
                                              x_sb[:, t, k * P:(k + 1) * P], ident[:, :])
                    mm.then_inc(turn_full, 1)
            ffn(0)

            def turn_blocks(u, blocks):
                pe.wait_ge(turned, u - 1)
                for i, blk in enumerate(blocks):
                    mm = pe.transpose(turn_ps[:, u % 2, i * P:(i + 1) * P], blk, ident[:, :])
                mm.then_inc(turn_full, 1)

            def turn_rows(u, src, tiles):
                turn_blocks(u, [src[:, t, k * P:(k + 1) * P] for k in tiles for t in range(TOK)])

            def turn_ws():
                pe.wait_ge(ws_landed, 16)
                for b in range(2):
                    turn_blocks(TWS + b, [ws_raw[:, 4 * b + i, :] for i in range(4)])

            def turn_qk(g):
                pe.wait_ge(qk_scaled, g + 1)
                src = q_sb if g < 2 else k_sb
                for b in range(2):
                    h = 4 * (g % 2) + 2 * b
                    turn_rows(TQK + 2 * g + b, src, (h, h + 1))

            def scores(h):
                pe.wait_ge(turned, TQK + 8)
                if h:
                    pe.wait_ge(max_ready, h)
                pe.matmul(y_ps[:, 0, 0:P], qt[:, h, 0:P], kt[:, h, 0:P], start=True, stop=True)
                pe.matmul(y_ps[:, 0, P:3 * P], qt[:, h, P:2 * P], kt[:, h, :],
                          start=True, stop=True).then_inc(s_done, 1)

            def turn_p(h):
                pe.wait_ge(p_ready, 2 * h + 2)
                turn_blocks(TP + h, [s_sb[:, h % 2, i * P:(i + 1) * P] for i in range(3)])

            def values(h):
                pe.wait_ge(turned, TP + h + 1)
                if h:
                    pe.wait_ge(o_taken, h)
                pe.wait_ge(proj_taken, 2 * 6 if h >= 4 else 2 * 5)
                v = [v_sb[:, t, h * HD:(h + 1) * HD] for t in range(TOK)]
                pe.matmul(y_ps[:, 1, 0:P], pt[:, h % 2, 0:P], v[0], start=True, stop=True)
                pe.matmul(y_ps[:, 1, P:2 * P], pt[:, h % 2, P:2 * P], v[0], start=True, stop=False)
                pe.matmul(y_ps[:, 1, P:2 * P], pt[:, h % 2, 2 * P:3 * P], v[1],
                          start=False, stop=True).then_inc(o_done, 1)

            def turn_attn(i):
                pe.wait_ge(attn_scaled, 2)
                for b in range(2):
                    turn_rows(TAT + 2 * i + b, q_sb, (4 * i + 2 * b, 4 * i + 2 * b + 1))

            def spatial(i):
                pe.wait_ge(ws_masked, 1)
                pe.wait_ge(ln_ready, 2 * i + 2)
                pe.wait_ge(o_taken, HEADS)
                if i:
                    pe.wait_ge(mixed_taken, 2)
                for t in range(TOK):
                    for g in range(4 * i, 4 * i + 4):
                        mm = pe.matmul(y_ps[:, t, (g % 4) * P:(g % 4 + 1) * P], wst[:, g, :],
                                       k_sb[:, t, g * P:(g + 1) * P], start=True, stop=True)
                    mm.then_inc(mixed_done, 1)

            def turn_sgu(i):
                pe.wait_ge(sgu_scaled, 2)
                for b in range(2):
                    turn_rows(TSG + 2 * i + b, k_sb, (4 * i + 2 * b, 4 * i + 2 * b + 1))

            jobs = {1: [lambda: turn_stage(TY1 + 2 * (XG - 1), x_ready, 2 * XG)], 8: [turn_ws],
                    66: [lambda: turn_attn(0), lambda: spatial(0)], 67: [lambda: turn_attn(1)],
                    74: [lambda: spatial(1)], 82: [lambda: turn_sgu(0)], 83: [lambda: turn_sgu(1)]}
            for g in range(4):
                jobs.setdefault(12 + 8 * g, []).append(lambda g=g: turn_qk(g))
            for h in range(HEADS):
                jobs.setdefault(40 + 2 * h, []).append(lambda h=h: scores(h))
                jobs.setdefault(43 + 2 * h, []).append(lambda h=h: turn_p(h))
                jobs.setdefault(45 + 2 * h, []).append(lambda h=h: values(h))

            for m in range(PG * ND):
                g, j = m // ND, m % ND
                k0, kn = HALVES_D[j]
                if m == 0:
                    pe.wait_ge(turned, TY1 + 2 * (XG - 1))
                if m == 6:
                    pe.wait_ge(turned, TY1 + 2 * XG)
                half(IN0 + m, j, k0, kn, xt_hi, xt_lo, psum_of[g % 2], KT - 1, proj_done,
                     (proj_taken, 2 * (g - 2)) if g >= 2 and j == 0 else None)
                for job in jobs.get(m, []):
                    job()

            def out_group(g, job, first=False):
                for j, (k0, kn) in enumerate(HALVES_D):
                    if first and k0 in (0, KT // 2, KT // 2 + 4):
                        pe.wait_ge(turned, {0: TAT + 4, KT // 2: TSG + 2, KT // 2 + 4: TSG + 4}[k0])
                    if first and j == 0:
                        pe.wait_ge(mixed_taken, 4)
                    half(OUT0 + g * ND + j, j, k0, kn, mt_hi, mt_lo, y_ps, KT - 1, y_done,
                         (x_ready, 2 * (XG + g - 1)) if j == 0 and not first else None)
                    job(j)

            out_group(0, lambda j: [f() for f in jobs.get(PG * ND + j, [])], first=True)
            with pe.Fori(1, XG) as g:
                out_group(g, lambda j: turn_stage(TY2 + 2 * (g - 1), x_ready, 2 * (XG + g - 1) + 2)
                          if j == 1 else None)
            ffn(1)

        @block.scalar
        def _(act):
            def round_high(n, j, kn, uses, first=False):
                slot = (j // 2) % RAW
                if j % 2 == 0:
                    act.wait_ge(raw_landed[slot], 16 * uses + 16)
                if not first:
                    act.wait_ge(split_used, n - SPL + 1)
                act.activation(w_hi[:, j % SPL, 0:kn * NCOL],
                               raw[:, slot, (j % 2) * 2 * NCOL:((j % 2) * 2 + kn) * NCOL],
                               ACT.Copy).then_inc(hi_ready, 1)

            def split_x(u, k, row, dst, tiles=2):
                act.wait_ge(turn_full, u + 1)
                for kk in range(2):
                    ins = act.activation(dst[:, bass.ds(k + kk, 1), :] if not isinstance(k, int) else dst[:, k + kk, :],
                                         turn_ps[:, u_bank(u), kk * 256:(kk + 1) * 256],
                                         ACT.Copy, scale=vec[:, bass.ds(row + k + kk, 1)])
                ins.then_inc(turn_high, 1)

            def u_bank(u):
                return bank_of[0]

            bank_of = [0]

            def split_group(u0, g, row, dst):
                for b in range(2):
                    bank_of[0] = b
                    split_x(u0 + b, 4 * g + 2 * b, row, dst)

            def split_gated(f, c):
                for b in range(2):
                    act.wait_ge(turn_full, TA[f] + 2 * c + b + 1)
                    act.activation(at_hi[f][:, bass.ds(4 * c + 2 * b, 2), :],
                                   turn_ps[:, b, :].rearrange("p (k t) -> p k t", k=2),
                                   ACT.Copy).then_inc(turn_high, 1)

            def silu(f, c):
                for t in range(TOK):
                    sum_done(act, gate_done, CHUNKS * f + c, GU0[f] + 2 * ND * c + ND - 1, t)
                    act.activation(stage[:, t, :], gate_ps[:, t, :], ACT.Silu,
                                   scale=root[:, ROOTS.index(["ffn1", "ffn2"][f]), t:t + 1]).then_inc(gate_taken, 1)

            def gate_up(f, c, job, first=False):
                n = GU0[f] + c * 2 * ND
                uses = GU0[f] // (2 * RAW) + c * 2
                for j, (_, kn) in enumerate(HALVES_D):
                    round_high(n + j, j, kn, uses, first and j < SPL)
                    if j == 5:
                        job()
                for j, (_, kn) in enumerate(HALVES_D):
                    round_high(n + ND + j, j, kn, uses + 1)
                    if j == 2:
                        silu(f, c)

            def down(f, g, job):
                for j, (_, kn) in enumerate(HALVES_F):
                    round_high(DN0[f] + g * NF + j, j, kn, DN0[f] // (2 * RAW) + g * 3 + j // (2 * RAW))
                    if j == 5:
                        job()

            def ffn(f):
                if f:
                    def job():
                        split_group(TY2 + 2 * (XG - 1), XG - 1, V_FFN2, xt_hi)
                        act.wait_ge(x_saved, 2 * XG)
                        act.wait_ge(root_ready, ROOTS.index("ffn2") + 1)
                    gate_up(1, 0, job)
                else:
                    gate_up(0, 0, lambda: act.wait_ge(root_ready, 1), first=True)
                with act.Fori(1, CHUNKS) as c:
                    gate_up(f, c, lambda: split_gated(f, c - 1))
                down(f, 0, lambda: split_gated(f, CHUNKS - 1))
                with act.Fori(1, XG) as g:
                    down(f, g, (lambda: None) if f else (lambda: split_group(TY1 + 2 * (g - 1), g - 1, V_MIX, xt_hi)))

            r = 0
            for src in (ffn1_norm, mix_norm, ffn2_norm, attn_out_gain, sgu_out_gain, q_norm, k_norm):
                rows = src[0].rearrange("(k p) -> k p", p=P)
                act.dma_start(vec_rows[r:r + rows.shape[0], :], rows).then_inc(vec_landed, 16)
                r += rows.shape[0]
            act.dma_start(vec_rows[r:r + SGU_G, :], sgu_b_spatial[0]).then_inc(vec_landed, 16)
            for g in range(XG):
                act.dma_start(x_sb[:, :, g * NCOL:(g + 1) * NCOL],
                              x_rows[:, :, g * NCOL:(g + 1) * NCOL]).then_inc(x_landed[g], 16)
            act.wait_ge(vec_ready, 1)
            for g in range(XG):
                split_group(TX0 + 2 * g, g, V_FFN1, xt_hi)
            ffn(0)

            root_mix = root[:, ROOTS.index("mix"), :]

            def take(g):
                dst = [q_sb, k_sb, v_sb, k_sb, None][g // 2]
                c = (g % 2) * NCOL
                if g == 9:
                    act.wait_ge(gated_u, 2)
                for t in range(TOK):
                    sum_done(act, proj_done, g, IN0 + ND * g + ND - 1, t)
                    to = stage[:, t, :] if dst is None else dst[:, t, c:c + NCOL]
                    act.activation(to, psum_of[g % 2][:, t, :], ACT.Gelu_apprx_tanh if g >= 6 else ACT.Copy,
                                   scale=root_mix[:, t:t + 1]).then_inc(proj_taken, 1)

            def exps(h):
                act.wait_ge(max_ready, h + 1)
                for t, (a, b) in enumerate(((0, P), (P, 3 * P))):
                    act.activation(s_sb[:, h % 2, a:b], s_sb[:, h % 2, a:b], ACT.Exp, bias=neg_max[:, h, t:t + 1],
                                   accum_out=row_sum[:, h, t:t + 1]).then_inc(p_ready, 1)

            def split_mixed(u, k, row):
                bank_of[0] = u % 2
                act.wait_ge(turn_full, u + 1)
                for kk in range(2):
                    ins = act.activation(mt_hi[:, k + kk, :], turn_ps[:, u % 2, kk * 256:(kk + 1) * 256],
                                         ACT.Copy, scale=vec[:, row + kk:row + kk + 1])
                ins.then_inc(turn_high, 1)

            def x_job():
                split_group(TY1 + 2 * (XG - 1), XG - 1, V_MIX, xt_hi)
                act.wait_ge(root_ready, ROOTS.index("mix") + 1)

            jobs = {5: [x_job]}
            for g, m in enumerate((10, 18, 26, 34, 42, 50, 59, 66, 74, 82)):
                jobs.setdefault(m, []).append(lambda g=g: take(g))
            for h in range(HEADS):
                jobs.setdefault(44 + 2 * h, []).append(lambda h=h: exps(h))
            for i in range(4):
                jobs.setdefault(69 + i // 2, []).append(lambda i=i: split_mixed(TAT + i, 2 * i, V_ATT + 2 * i))
                jobs.setdefault(85 + i // 2, []).append(
                    lambda i=i: split_mixed(TSG + i, KT // 2 + 2 * i, V_SGU + 2 * i))

            for m in range(PG * ND):
                g, j = m // ND, m % ND
                round_high(IN0 + m, j, 2, IN0 // (2 * RAW) + g)
                for job in jobs.get(m, []):
                    job()

            def out_group(g, job):
                for j in range(ND):
                    round_high(OUT0 + g * ND + j, j, 2, OUT0 // (2 * RAW) + g)
                    job(j)

            out_group(0, lambda j: [f() for f in jobs.get(PG * ND + j, [])])
            with act.Fori(1, XG) as g:
                out_group(g, lambda j: split_group(TY2 + 2 * (g - 1), g - 1, V_FFN2, xt_hi) if j == 5 else None)
            ffn(1)

        @block.vector
        def _(dve):
            steps = [0]

            def link(ins):
                steps[0] += 1
                ins.then_inc(dve_step, 1)
                dve.wait_ge(dve_step, steps[0])

            def rest_low(n, j, kn):
                slot = (j // 2) % RAW
                dve.wait_ge(hi_ready, n + 1)
                dve.tensor_tensor(w_lo[:, j % SPL, 0:kn * NCOL],
                                  raw[:, slot, (j % 2) * 2 * NCOL:((j % 2) * 2 + kn) * NCOL],
                                  w_hi[:, j % SPL, 0:kn * NCOL].bitcast(F32), ALU.subtract).then_inc(lo_ready, 1)

            def split_group(s0, g, row):
                for b in range(2):
                    dve.wait_ge(turn_high, s0 + b + 1)
                    for kk in range(2):
                        k = 4 * g + 2 * b + kk
                        ins = dve.scalar_tensor_tensor(
                            out=xt_lo[:, bass.ds(k, 1), :], in0=turn_ps[:, b:b + 1, kk * 256:(kk + 1) * 256],
                            scalar=vec[:, bass.ds(row + k, 1)], in1=xt_hi[:, bass.ds(k, 1), :].bitcast(F32),
                            op0=ALU.mult, op1=ALU.subtract)
                    ins.then_inc(turned, 1)

            def split_gated(f, c):
                for b in range(2):
                    dve.wait_ge(turn_high, SA[f] + 2 * c + b + 1)
                    k = bass.ds(4 * c + 2 * b, 2)
                    dve.tensor_tensor(at_lo[f][:, k, :], turn_ps[:, b, :].rearrange("p (k t) -> p k t", k=2),
                                      at_hi[f][:, k, :].bitcast(F32), ALU.subtract).then_inc(turned, 1)

            def gated(f, c):
                for t in range(TOK):
                    dve.wait_ge(gate_taken, 2 * (CHUNKS * f + c) + t + 1)
                    sum_done(dve, up_done, CHUNKS * f + c, GU0[f] + 2 * ND * c + 2 * ND - 1, t)
                    dve.scalar_tensor_tensor(out=stage[:, t, :], in0=up_ps[:, t, :],
                                             scalar=root[:, ROOTS.index(["ffn1", "ffn2"][f]), t:t + 1],
                                             in1=stage[:, t, :], op0=ALU.mult, op1=ALU.mult).then_inc(gated_ready, 1)

            def add_x(y, g, scale, last_half, last=False, first_of=False):
                for t in range(TOK):
                    sum_done(dve, y_done, y, last_half, t)
                    if last and not first_of:
                        dve.wait_ge(out_landed[t], 16 * g)
                    dve.scalar_tensor_tensor(out=stage[:, t, :], in0=y_ps[:, t, :], scalar=scale,
                                             in1=x_sb[:, t, bass.ts(g, NCOL)], op0=ALU.mult, op1=ALU.add)\
                       .then_inc(x_ready, 1)
                    if not last:
                        dve.wait_ge(x_ready, 2 * y + t + 1)
                        dve.bn_stats(stats[:, t, g, :] if isinstance(g, int) else stats[:, t, bass.ds(g, 1), :],
                                     stage[:, t, :]).then_inc(dve_step, 1)

            def mean_square(name, src, n, link_first=True):
                i = ROOTS.index(name)
                for t in range(TOK):
                    link(dve.bn_aggr(agg[:, t, :], src[:, t, 0:n, :].rearrange("p a b -> p (a b)")))
                link(dve.tensor_tensor(mean_sq[:, i, 0:2], agg[:, :, 0], agg[:, :, 0], ALU.mult))
                dve.scalar_tensor_tensor(out=mean_sq[:, i, 0:2], in0=mean_sq[:, i, 0:2], scalar=EPS, in1=agg[:, :, 1],
                                         op0=ALU.add, op1=ALU.add).then_inc(ms_ready, 1)

            def gate_up(f, c, jobs):
                n = GU0[f] + c * 2 * ND
                for j, (_, kn) in enumerate(HALVES_D + HALVES_D):
                    rest_low(n + j, j, kn)
                    if j in jobs:
                        jobs[j]()

            def down(f, g, jobs):
                for j, (_, kn) in enumerate(HALVES_F):
                    rest_low(DN0[f] + g * NF + j, j, kn)
                    if j in jobs:
                        jobs[j]()

            def ffn(f):
                y0 = 2 * XG * f
                if f:
                    def end_x():
                        dve.wait_ge(x_saved, 2 * XG - 1)
                        add_x(2 * XG - 1, XG - 1, 1.0, GU0[1] - 1)
                        steps[0] += 2
                        dve.wait_ge(dve_step, steps[0])
                        mean_square("ffn2", stats, XG)
                    gate_up(1, 0, {2: end_x, 5: lambda: split_group(SY2 + 2 * (XG - 1), XG - 1, V_FFN2),
                                   6: lambda: dve.wait_ge(root_ready, ROOTS.index("ffn2") + 1)})
                else:
                    gate_up(0, 0, {6: lambda: dve.wait_ge(root_ready, 1)})
                with dve.Fori(1, CHUNKS) as c:
                    gate_up(f, c, {2: lambda: gated(f, c - 1), 5: lambda: split_gated(f, c - 1)})
                down(f, 0, {2: lambda: gated(f, CHUNKS - 1), 5: lambda: split_gated(f, CHUNKS - 1)})
                if f:
                    down(f, 1, {2: lambda: add_x(y0, 0, 0.5, DN0[f] + NF - 1, last=True, first_of=True)})
                    with dve.Fori(2, XG) as g:
                        down(f, g, {2: lambda: add_x(y0 + g - 1, g - 1, 0.5, DN0[f] + NF * g - 1, last=True)})
                    add_x(y0 + XG - 1, XG - 1, 0.5, DN0[f] + NF * XG - 1, last=True)
                else:
                    def job0():
                        add_x(0, 0, 0.5, DN0[f] + NF - 1)
                    down(f, 1, {2: job0, 5: lambda: split_group(SY1, 0, V_MIX)})

                    with dve.Fori(2, XG) as g:
                        def job(g=g):
                            dve.wait_ge(x_saved, g - 1)
                            add_x(g - 1, g - 1, 0.5, DN0[f] + NF * g - 1)
                        down(f, g, {2: job, 5: lambda: split_group(SY1 + 2 * (g - 1), g - 1, V_MIX)})
                    steps[0] += 2 * (XG - 1)

            dve.memset(neg_half[:, :], -0.5).then_inc(ident_ready, 1)
            dve.wait_ge(vec_turned, 1)
            dve.tensor_copy(vec[:, :], y_ps[:, 0, 0:NVEC]).then_inc(vec_ready, 1)
            dve.wait_ge(vec_ready, 1)
            for g in range(XG):
                dve.wait_ge(x_landed[g], 16)
                for t in range(TOK):
                    dve.bn_stats(stats[:, t, g, :], x_sb[:, t, g * NCOL:(g + 1) * NCOL]).then_inc(dve_step, 1)
                    steps[0] += 1
                split_group(SX0 + 2 * g, g, V_FFN1)
            dve.wait_ge(dve_step, steps[0])
            mean_square("ffn1", stats, XG)
            ffn(0)

            def copy_ws():
                for b in range(2):
                    dve.wait_ge(turn_full, TWS + b + 1)
                    dve.tensor_copy(wst[:, 4 * b:4 * b + 4, :],
                                    turn_ps[:, b, :].rearrange("p (g t) -> p g t", t=P)).then_inc(turned, 1)

            def end_x():
                dve.wait_ge(x_saved, XG - 1)
                add_x(XG - 1, XG - 1, 0.5, IN0 - 1)
                steps[0] += 2
                dve.wait_ge(dve_step, steps[0])
                mean_square("mix", stats, XG)

            def qk_squares(g):
                src = q_sb if g < 2 else k_sb
                c = (g % 2) * NCOL
                if g == 0:
                    dve.wait_ge(x_saved, XG)
                for t in range(TOK):
                    dve.wait_ge(proj_taken, 2 * g + t + 1)
                    link(dve.tensor_tensor(stage[:, t, :], src[:, t, c:c + NCOL], src[:, t, c:c + NCOL], ALU.mult))
                    link(dve.tensor_reduce(sq_sum[:, t, :], stage[:, t, :].rearrange("p (h d) -> p h d", d=HD),
                                           AXX, ALU.add))
                dve.tensor_scalar(mean_sq[:, ROOTS.index(f"qk{g}"), :], sq_sum[:, :, :].rearrange("p t h -> p (t h)"),
                                  1.0 / HD, EPS, ALU.mult, ALU.add).then_inc(ms_ready, 1)

            def qk_scale(g):
                src = q_sb if g < 2 else k_sb
                c = (g % 2) * NCOL
                i = ROOTS.index(f"qk{g}")
                dve.wait_ge(root_ready, i + 1)
                for t in range(TOK):
                    v = src[:, t, c:c + NCOL].rearrange("p (h d) -> p h d", d=HD)
                    ins = dve.tensor_tensor(v, v, root[:, i, 4 * t:4 * t + 4, None].to_broadcast([P, 4, HD]), ALU.mult)
                ins.then_inc(qk_scaled, 1)

            def qk_turned(g):
                dst, col = (qt, V_Q) if g < 2 else (kt, V_K)
                for b in range(2):
                    h = 4 * (g % 2) + 2 * b
                    dve.wait_ge(turn_full, TQK + 2 * g + b + 1)
                    dve.tensor_scalar(dst[:, h:h + 2, :], turn_ps[:, b, :].rearrange("p (h t) -> p h t", h=2),
                                      vec[:, col:col + 1], None, ALU.mult).then_inc(turned, 1)

            def masked_max(h):
                dve.wait_ge(s_done, h + 1)
                if h == 0:
                    dve.wait_ge(mask_ready, 1)
                if h >= 2:
                    dve.wait_ge(turn_full, TP + h - 1)
                link(dve.scalar_tensor_tensor(out=s_sb[:, h % 2, :], in0=y_ps[:, 0, 0:3 * P], scalar=SCALE,
                                              in1=mask[:, :], op0=ALU.mult, op1=ALU.add))
                dve.tensor_reduce(neg_max[:, h, 0:1], s_sb[:, h % 2, 0:P], AXX, ALU.max, negate=True)
                dve.tensor_reduce(neg_max[:, h, 1:2], s_sb[:, h % 2, P:3 * P], AXX, ALU.max,
                                  negate=True).then_inc(max_ready, 1)

            def take_p(h):
                dve.wait_ge(p_ready, 2 * h + 2)
                dve.wait_ge(turn_full, TP + h + 1)
                if h >= 2:
                    dve.wait_ge(o_done, h - 1)
                dve.tensor_copy(pt[:, h % 2, :], turn_ps[:, (TP + h) % 2, 0:3 * P]).then_inc(turned, 1)
                link(dve.reciprocal(inv_sum[:, h, :], row_sum[:, h, :]))

            def take_o(h):
                dve.wait_ge(o_done, h + 1)
                for t in range(TOK):
                    ins = dve.tensor_scalar(q_sb[:, t, h * HD:(h + 1) * HD], y_ps[:, 1, t * P:(t + 1) * P],
                                            inv_sum[:, h, t:t + 1], None, ALU.mult)
                ins.then_inc(o_taken, 1)

            def row_stats(src):
                for c in range(2):
                    for t in range(TOK):
                        ins = dve.bn_stats(stats[:, t, c, :], src[:, t, c * NCOL:(c + 1) * NCOL])
                link(ins)

            def attn_square():
                dve.wait_ge(o_taken, HEADS)
                row_stats(q_sb)
                mean_square("attn", stats, 2)

            def scale_rows(name, src, done):
                i = ROOTS.index(name)
                dve.wait_ge(root_ready, i + 1)
                for t in range(TOK):
                    dve.tensor_scalar(src[:, t, :], src[:, t, :], root[:, i, t:t + 1], None, ALU.mult).then_inc(done, 1)

            def split_mixed(u, s, k, row):
                dve.wait_ge(turn_high, s + 1)
                for kk in range(2):
                    ins = dve.scalar_tensor_tensor(
                        out=mt_lo[:, k + kk, :], in0=turn_ps[:, u % 2, kk * 256:(kk + 1) * 256],
                        scalar=vec[:, row + kk:row + kk + 1], in1=mt_hi[:, k + kk, :].bitcast(F32),
                        op0=ALU.mult, op1=ALU.subtract)
                ins.then_inc(turned, 1)

            def ln_square(i):
                for t in range(TOK):
                    dve.wait_ge(proj_taken, 2 * (6 + i) + t + 1)
                    for g in range(4):
                        ins = dve.bn_stats(ln_stats[:, t, g, :], k_sb[:, t, (4 * i + g) * P:(4 * i + g + 1) * P])
                link(ins)
                for t in range(TOK):
                    for g in range(4):
                        ins = dve.bn_aggr(ln_agg[:, t, g, :], ln_stats[:, t, g, :])
                link(ins)
                dve.tensor_scalar(mean_sq[:, ROOTS.index(f"ln{i}"), :].rearrange("p (t g) -> p t g", t=2),
                                  ln_agg[:, :, :, 1], EPS, None, ALU.add).then_inc(ms_ready, 1)

            def ln_scale(i, t):
                r = ROOTS.index(f"ln{i}")
                dve.wait_ge(root_ready, r + 1)
                dve.wait_ge(ln_landed, 32)
                for g in range(4):
                    v = k_sb[:, t, (4 * i + g) * P:(4 * i + g + 1) * P]
                    ins = dve.tensor_scalar(v, v, ln_agg[:, t, g, 0:1], root[:, r, 4 * t + g:4 * t + g + 1],
                                            ALU.subtract, ALU.mult)
                link(ins)
                v = k_sb[:, t, i * NCOL:(i + 1) * NCOL]
                link(dve.tensor_tensor(v, v, ln_rows[:, 0, i * NCOL:(i + 1) * NCOL], ALU.mult))
                dve.tensor_tensor(v, v, ln_rows[:, 1, i * NCOL:(i + 1) * NCOL], ALU.add).then_inc(ln_ready, 1)

            def take_mixed(i):
                for t in range(TOK):
                    dve.wait_ge(mixed_done, 2 * i + 2)
                    dve.tensor_tensor(k_sb[:, t, i * NCOL:(i + 1) * NCOL].rearrange("p (g c) -> p g c", c=P),
                                      y_ps[:, t, :].rearrange("p (g c) -> p g c", c=P),
                                      vec[:, V_BS + 4 * i:V_BS + 4 * i + 4, None].to_broadcast([P, 4, P]),
                                      ALU.add).then_inc(mixed_taken, 1)

            def gate_u(i):
                for t in range(TOK):
                    dve.wait_ge(proj_taken, 2 * (8 + i) + t + 1)
                    dve.wait_ge(mixed_taken, 2 * i + t + 1)
                    v = k_sb[:, t, i * NCOL:(i + 1) * NCOL]
                    dve.tensor_tensor(v, v, stage[:, t, :], ALU.mult).then_inc(gated_u, 1)

            def sgu_square():
                dve.wait_ge(gated_u, 4)
                row_stats(k_sb)
                mean_square("sgu", stats, 2)

            jobs = {2: [end_x], 5: [lambda: split_group(SY1 + 2 * (XG - 1), XG - 1, V_MIX)], 11: [copy_ws],
                    61: [lambda: ln_square(0)], 62: [lambda: ln_scale(0, 0)], 63: [lambda: ln_scale(0, 1)],
                    64: [attn_square], 65: [lambda: scale_rows("attn", q_sb, attn_scaled)],
                    67: [lambda: ln_square(1)], 71: [lambda: ln_scale(1, 0)], 72: [lambda: ln_scale(1, 1)],
                    68: [lambda: take_mixed(0)], 76: [lambda: gate_u(0)], 77: [lambda: take_mixed(1)],
                    82: [lambda: gate_u(1), sgu_square], 83: [lambda: scale_rows("sgu", k_sb, sgu_scaled)]}
            for g in range(4):
                jobs.setdefault(11 + 8 * g, []).append(lambda g=g: qk_squares(g))
                jobs.setdefault(13 + 8 * g, []).append(lambda g=g: qk_scale(g))
                jobs.setdefault(15 + 8 * g, []).append(lambda g=g: qk_turned(g))
            for h in range(HEADS):
                jobs.setdefault(43 + 2 * h, []).append(lambda h=h: masked_max(h))
                jobs.setdefault(46 + 2 * h, []).append(lambda h=h: take_p(h))
                jobs.setdefault(48 + 2 * h, []).append(lambda h=h: take_o(h))
            for i in range(4):
                jobs.setdefault(69 + i // 2, []).append(
                    lambda i=i: split_mixed(TAT + i, SAT + i, 2 * i, V_ATT + 2 * i))
                jobs.setdefault(85 + i // 2, []).append(
                    lambda i=i: split_mixed(TSG + i, SSG + i, KT // 2 + 2 * i, V_SGU + 2 * i))

            for m in range(PG * ND):
                rest_low(IN0 + m, m % ND, 2)
                for job in jobs.get(m, []):
                    job()

            def out_group(g, jobs_of):
                for j in range(ND):
                    rest_low(OUT0 + g * ND + j, j, 2)
                    for job in jobs_of.get(j, []):
                        job()

            out_group(0, {j: jobs.get(PG * ND + j, []) for j in range(ND)})
            with dve.Fori(1, XG) as g:
                def job(g=g):
                    dve.wait_ge(x_saved, XG + g - 1)
                    add_x(XG + g - 1, g - 1, 1.0, OUT0 + ND * g - 1)
                out_group(g, {2: [job], 5: [lambda: split_group(SY2 + 2 * (g - 1), g - 1, V_FFN2)]})
            steps[0] += 2 * (XG - 1)
            ffn(1)

        @block.gpsimd
        def _(pool):
            pool.memset(ident[:, :], 0.0).then_inc(pool_step, 1)
            pool.wait_ge(pool_step, 1)
            pool.affine_select(out=ident[:, :], in_=ident[:, :], compare_op=ALU.not_equal, fill=1.0, base=0,
                               pattern=[[-1, P]], channel_multiplier=1).then_inc(ident_ready, 1)

            def roots(name, n=2):
                i = ROOTS.index(name)
                pool.wait_ge(ms_ready, i + 1)
                pool.tensor_tensor(root[:, i, 0:n], mean_sq[:, i, 0:n], neg_half[:, 0:n], ALU.pow)\
                    .then_inc(root_ready, 1)

            def save_x(y, g):
                pool.wait_ge(x_ready, 2 * y + 2)
                pool.tensor_copy(x_sb[:, :, bass.ts(g, NCOL)], stage[:, :, :]).then_inc(x_saved, 1)

            pool.wait_ge(ident_ready, 2)
            roots("ffn1")
            with pool.Fori(0, XG) as g:
                save_x(g, g)
            roots("mix")

            pool.wait_ge(split_used, IN0)
            pool.dma_start(ws_raw, sgu_w_spatial[0].rearrange("g t s -> t g s")).then_inc(ws_landed, 16)
            pool.memset(mask[:, :], 0.0).then_inc(pool_step, 1)
            pool.wait_ge(pool_step, 2)
            for n, a in enumerate((0, 2 * P)):
                pool.affine_select(out=mask[:, a:a + P], in_=mask[:, a:a + P], compare_op=ALU.is_ge, fill=NEG,
                                   base=0, pattern=[[-1, P]], channel_multiplier=1).then_inc(pool_step, 1)
            pool.wait_ge(pool_step, 4)
            pool.sem_inc(mask_ready, 1)
            roots("qk0", 8)
            pool.wait_ge(turned, TWS + 2)
            pool.affine_select(out=wst[:, :, :], in_=wst[:, :, :], compare_op=ALU.is_ge, fill=0.0, base=0,
                               pattern=[[0, SGU_G], [1, P]], channel_multiplier=-1).then_inc(ws_masked, 1)
            for g in range(1, 4):
                roots(f"qk{g}", 8)
            pool.wait_ge(s_done, HEADS)
            for i, v in enumerate((sgu_ln_gain, sgu_ln_bias)):
                pool.dma_start(ln_rows[:, i, :], v[0].rearrange("(a n) -> a n", a=1).to_broadcast([P, DATT]))\
                    .then_inc(ln_landed, 16)
            roots("ln0", 8)
            roots("attn")
            roots("ln1", 8)
            roots("sgu")
            with pool.Fori(0, XG) as g:
                save_x(XG + g, g)
            roots("ffn2")
            with pool.Fori(0, XG) as g:
                for t in range(TOK):
                    pool.wait_ge(x_ready, 4 * XG + 2 * g + t + 1)
                    pool.dma_start(out_rows[:, t, bass.ts(g, NCOL)], stage[:, t, :]).then_inc(out_landed[t], 16)
            for t in range(TOK):
                pool.wait_ge(out_landed[t], 16 * XG)


_INS = ["x", "ffn1_norm", "ffn1_w_gate", "ffn1_w_up", "ffn1_w_down", "mix_norm", "w_in", "q_norm", "k_norm",
        "sgu_ln_gain", "sgu_ln_bias", "sgu_w_spatial", "sgu_b_spatial", "attn_out_gain", "sgu_out_gain", "w_out",
        "ffn2_norm", "ffn2_w_gate", "ffn2_w_up", "ffn2_w_down"]


def kernel(**inputs):
    import numpy as np
    import concourse.bacc as bacc
    from concourse import mybir as mb
    from concourse.bass_utils import run_bass_kernel_spmd

    nc = bacc.Bacc("TRN2", target_bir_lowering=False, num_devices=1)
    arrays, args = {}, []
    for name in _INS:
        a = np.ascontiguousarray(inputs[name])
        arrays[f"in_{name}"] = a
        args.append(nc.dram_tensor(f"in_{name}", a.shape, mb.dt.from_np(a.dtype), kind="ExternalInput").ap())
    shape = tuple(inputs["x"].shape)
    args.append(nc.dram_tensor("out_x", shape, mb.dt.float32, kind="ExternalOutput").ap())
    build(nc, *args)
    r = run_bass_kernel_spmd(nc, [arrays], core_ids=[0])
    return r.results[0]["out_x"]
```

```python
from contextlib import ExitStack

import concourse.bass as bass
from concourse import mybir

ALU = mybir.AluOpType
ACT = mybir.ActivationFunctionType
AXX = mybir.AxisListType.X
F32 = mybir.dt.float32
F32R = mybir.dt.float32r

P = 128
NCOL = 512
TOK = 2
D = 2048
DFF = 5632
HEADS = 8
HD = 128
DATT = HEADS * HD
SGU_G = 8
KT = D // P
FT = DFF // P
CHUNKS = DFF // NCOL
XG = D // NCOL
PG = (3 * DATT + 2 * DATT) // NCOL
RAW = 4
SPL = 4
EPS = 1e-6
SCALE = float(HD) ** -0.5
NEG = -1e30

HALVES_D = [(2 * j, 2) for j in range(KT // 2)]
HALVES_F = [(11 * (j // 6) + [0, 2, 4, 6, 8, 9][j % 6], 1 if j % 6 == 4 else 2) for j in range(24)]
assert sum(n for _, n in HALVES_F) == FT and D % P == 0
ND, NF = len(HALVES_D), len(HALVES_F)

IN0 = CHUNKS * 2 * ND + XG * NF
OUT0 = IN0 + PG * ND
GU0 = [0, OUT0 + XG * ND]
DN0 = [h + CHUNKS * 2 * ND for h in GU0]
assert all(h % (2 * RAW) == 0 for h in GU0 + DN0 + [IN0, OUT0])

TX0 = 0
TA = [TX0 + 2 * XG, 0]
TY1 = TA[0] + 2 * CHUNKS
TWS = TY1 + 2 * XG
TQK = TWS + 2
TP = TQK + 8
TAT = TP + HEADS
TSG = TAT + 4
TY2 = TSG + 4
TA[1] = TY2 + 2 * XG
SX0 = 0
SA = [SX0 + 2 * XG, 0]
SY1 = SA[0] + 2 * CHUNKS
SAT = SY1 + 2 * XG
SSG = SAT + 4
SY2 = SSG + 4
SA[1] = SY2 + 2 * XG

ROOTS = ["ffn1", "mix", "qk0", "qk1", "qk2", "qk3", "ln0", "attn", "ln1", "sgu", "ffn2"]

V_FFN1, V_MIX, V_FFN2, V_ATT, V_SGU, V_Q, V_K, V_BS = 0, 16, 32, 48, 56, 64, 65, 66
NVEC = 74


def build(nc, x, ffn1_norm, ffn1_w_gate, ffn1_w_up, ffn1_w_down, mix_norm, w_in, q_norm, k_norm,
          sgu_ln_gain, sgu_ln_bias, sgu_w_spatial, sgu_b_spatial, attn_out_gain, sgu_out_gain, w_out,
          ffn2_norm, ffn2_w_gate, ffn2_w_up, ffn2_w_down, out):
    w_gate = [ffn1_w_gate[0], ffn2_w_gate[0]]
    w_up = [ffn1_w_up[0], ffn2_w_up[0]]
    w_down = [ffn1_w_down[0], ffn2_w_down[0]]
    x_rows = x[0].rearrange("(t p) d -> p t d", p=P)
    out_rows = out[0].rearrange("(t p) d -> p t d", p=P)

    with ExitStack() as ctx:
        def sb(name, shape, dt=F32, where=ctx):
            return where.enter_context(nc.sbuf_tensor(name, shape, dt))

        def sem(name):
            return ctx.enter_context(nc.semaphore(name))

        x_sb = sb("x_sb", [P, TOK, D])
        xt_hi = sb("xt_hi", [P, KT, TOK * P], F32R)
        xt_lo = sb("xt_lo", [P, KT, TOK * P], F32R)
        raw = sb("raw", [P, RAW, 4 * NCOL])
        w_hi = sb("w_hi", [P, SPL, 2 * NCOL], F32R)
        w_lo = sb("w_lo", [P, SPL, 2 * NCOL], F32R)
        stage = sb("stage", [P, TOK, NCOL])
        ident = sb("ident", [P, P])
        vec = sb("vec", [P, NVEC])
        stats = sb("stats", [P, TOK, XG, 6])
        agg = sb("agg", [P, TOK, 2])
        mean_sq = sb("mean_sq", [P, len(ROOTS), 8])
        root = sb("root", [P, len(ROOTS), 8])
        neg_half = sb("neg_half", [P, 8])

        with ExitStack() as ffn:
            at1_hi = sb("at1_hi", [P, FT, TOK * P], F32R, ffn)
            at1_lo = sb("at1_lo", [P, FT, TOK * P], F32R, ffn)
        with ExitStack() as mixer:
            q_sb = sb("q_sb", [P, TOK, DATT], F32, mixer)
            k_sb = sb("k_sb", [P, TOK, DATT], F32, mixer)
            v_sb = sb("v_sb", [P, TOK, DATT], F32, mixer)
            qt = sb("qt", [P, HEADS, TOK * P], F32, mixer)
            kt = sb("kt", [P, HEADS, TOK * P], F32, mixer)
            mt_hi = sb("mt_hi", [P, KT, TOK * P], F32R, mixer)
            mt_lo = sb("mt_lo", [P, KT, TOK * P], F32R, mixer)
            wst = sb("wst", [P, SGU_G, P], F32, mixer)
            s_sb = sb("s_sb", [P, 2, 3 * P], F32, mixer)
            pt = sb("pt", [P, 2, 3 * P], F32, mixer)
            mask = sb("mask", [P, 3 * P], F32, mixer)
            sq_sum = sb("sq_sum", [P, TOK, 4], F32, mixer)
            neg_max = sb("neg_max", [P, HEADS, TOK], F32, mixer)
            row_sum = sb("row_sum", [P, HEADS, TOK], F32, mixer)
            inv_sum = sb("inv_sum", [P, HEADS, TOK], F32, mixer)
            ln_stats = sb("ln_stats", [P, TOK, 4, 6], F32, mixer)
            ln_agg = sb("ln_agg", [P, TOK, 4, 2], F32, mixer)
        with ExitStack() as ffn:
            at2_hi = sb("at2_hi", [P, FT, TOK * P], F32R, ffn)
            at2_lo = sb("at2_lo", [P, FT, TOK * P], F32R, ffn)
        at_hi, at_lo = [at1_hi, at2_hi], [at1_lo, at2_lo]
        vec_rows = stage[0:NVEC, :, 0:P]
        ws_raw = kt[:, 0:4, :].rearrange("p a (b s) -> p (a b) s", s=P)
        ln_rows = kt[:, :, :].rearrange("p h t -> p (h t)").rearrange("p (a c) -> p a c", a=2)

        gate_ps = ctx.enter_context(nc.psum_tensor("gate_ps", [P, TOK, NCOL], F32))
        up_ps = ctx.enter_context(nc.psum_tensor("up_ps", [P, TOK, NCOL], F32))
        y_ps = ctx.enter_context(nc.psum_tensor("y_ps", [P, TOK, NCOL], F32))
        turn_ps = ctx.enter_context(nc.psum_tensor("turn_ps", [P, 2, NCOL], F32))

        raw_landed = [sem(f"raw_landed{s}") for s in range(RAW)]
        hi_ready = sem("hi_ready")
        lo_ready = sem("lo_ready")
        split_used = sem("split_used")
        gate_done = sem("gate_done")
        gate_taken = sem("gate_taken")
        up_done = sem("up_done")
        gated_ready = sem("gated_ready")
        y_done = sem("y_done")
        x_ready = sem("x_ready")
        x_saved = sem("x_saved")
        turn_full = sem("turn_full")
        turn_high = sem("turn_high")
        turned = sem("turned")
        vec_landed, vecs_landed = sem("vec_landed"), sem("vecs_landed")
        x_landed = [sem(f"x_landed{g}") for g in range(XG)]
        ident_ready, vec_turned, vec_ready = sem("ident_ready"), sem("vec_turned"), sem("vec_ready")
        pool_step, dve_step = sem("pool_step"), sem("dve_step")
        ms_ready = sem("ms_ready")
        root_ready = sem("root_ready")
        proj_done = sem("proj_done")
        proj_taken = sem("proj_taken")
        qk_scaled = sem("qk_scaled")
        ws_landed, ws_masked, mask_ready = sem("ws_landed"), sem("ws_masked"), sem("mask_ready")
        ln_landed, ln_ready = sem("ln_landed"), sem("ln_ready")
        s_done, max_ready, p_ready = sem("s_done"), sem("max_ready"), sem("p_ready")
        o_done, o_taken = sem("o_done"), sem("o_taken")
        attn_scaled, sgu_scaled = sem("attn_scaled"), sem("sgu_scaled")
        mixed_done, mixed_taken = sem("mixed_done"), sem("mixed_taken")
        gated_u = sem("gated_u")
        out_landed = [sem(f"out_landed{t}") for t in range(TOK)]
        last_landed = sem("last_landed")

        def sum_done(eng, done, group, last_half, t):
            if t == 0:
                eng.wait_ge(done, group + 1)
            else:
                eng.wait_ge(split_used, last_half + 1)

        psum_of = [gate_ps, up_ps]
        block = ctx.enter_context(nc.Block())

        @block.sync
        def _(sp):
            def load(weights, col, halves, piece, j, first=False):
                k0 = halves[2 * j][0]
                n = halves[2 * j][1] + halves[2 * j + 1][1]
                if not first:
                    sp.wait_ge(lo_ready, 2 * piece - 2 * RAW + 2)
                src = weights[k0 * P:(k0 + n) * P, col].rearrange("(k p) n -> p k n", p=P)
                dst = raw[:, j % RAW, 0:n * NCOL].rearrange("p (k n) -> p k n", n=NCOL)
                sp.dma_start(dst, src).then_inc(raw_landed[j % RAW], 16)

            def gate_up(f, c, first=False):
                piece = GU0[f] // 2 + c * ND
                for j in range(ND // 2):
                    if first:
                        sp.dma_start(x_sb[:, :, j * NCOL:(j + 1) * NCOL],
                                     x_rows[:, :, j * NCOL:(j + 1) * NCOL]).then_inc(x_landed[j], 16)
                    load(w_gate[f], bass.ts(c, NCOL), HALVES_D, piece + j, j, first)
                for j in range(ND // 2):
                    load(w_up[f], bass.ts(c, NCOL), HALVES_D, piece + ND // 2 + j, j)

            def groups(weights, halves, start, n, shift=0):
                with sp.Fori(0, n) as g:
                    for j in range(len(halves) // 2):
                        load(weights, bass.ts(g + shift, NCOL), halves, start // 2 + g * (len(halves) // 2) + j, j)

            gate_up(0, 0, first=True)
            with sp.Fori(1, CHUNKS) as c:
                gate_up(0, c)
            groups(w_down[0], HALVES_F, DN0[0], XG)
            groups(w_in[0], HALVES_D, IN0, 6)
            groups(w_in[0], HALVES_D, IN0 + 6 * ND, 2, shift=8)
            groups(w_in[0], HALVES_D, IN0 + 8 * ND, 2, shift=6)
            groups(w_out[0], HALVES_D, OUT0, XG)
            with sp.Fori(0, CHUNKS) as c:
                gate_up(1, c)
            groups(w_down[1], HALVES_F, DN0[1], XG)
            for t in range(TOK):
                sp.wait_ge(x_ready, 4 * XG + 2 * (XG - 1) + t + 1)
                sp.dma_start(out_rows[:, t, (XG - 1) * NCOL:XG * NCOL], stage[:, t, :]).then_inc(last_landed, 16)
            sp.wait_ge(last_landed, 16 * TOK)

        @block.tensor
        def _(pe):
            def half(n, j, k0, kn, lhs_hi, lhs_lo, dst, last_k, done, free=None):
                pe.wait_ge(lo_ready, n + 1)
                for t in range(TOK):
                    if free is not None:
                        pe.wait_ge(free[0], free[1] + t + 1)
                    for k in range(k0, k0 + kn):
                        hi = w_hi[:, j % SPL, (k - k0) * NCOL:(k - k0 + 1) * NCOL]
                        lo = w_lo[:, j % SPL, (k - k0) * NCOL:(k - k0 + 1) * NCOL]
                        a_hi = lhs_hi[:, k, t * P:(t + 1) * P]
                        a_lo = lhs_lo[:, k, t * P:(t + 1) * P]
                        pe.matmul(dst[:, t, :], a_hi, hi, start=(k == 0), stop=False)
                        pe.matmul(dst[:, t, :], a_hi, lo, start=False, stop=False)
                        mm = pe.matmul(dst[:, t, :], a_lo, hi, start=False, stop=(k == last_k))
                    if k == last_k and t == 0:
                        mm.then_inc(done, 1)
                mm.then_inc(split_used, 1)

            def turn_stage(u, ready, value):
                pe.wait_ge(ready, value)
                for b in range(2):
                    pe.wait_ge(turned, u + b - 1)
                    for kk in range(2):
                        for t in range(TOK):
                            mm = pe.transpose(turn_ps[:, b, kk * 256 + t * P:kk * 256 + (t + 1) * P],
                                              stage[:, t, (2 * b + kk) * P:(2 * b + kk + 1) * P], ident[:, :])
                    mm.then_inc(turn_full, 1)

            def turn_x(g):
                pe.wait_ge(x_landed[g], 16)
                for b in range(2):
                    u = TX0 + 2 * g + b
                    if u >= 2:
                        pe.wait_ge(turned, u - 1)
                    for kk in range(2):
                        k = 4 * g + 2 * b + kk
                        for t in range(TOK):
                            mm = pe.transpose(turn_ps[:, b, kk * 256 + t * P:kk * 256 + (t + 1) * P],
                                              x_sb[:, t, k * P:(k + 1) * P], ident[:, :])
                    mm.then_inc(turn_full, 1)

            def turn_vectors():
                pe.wait_ge(vecs_landed, 16 * 7)
                pe.transpose(y_ps[:, 0, KT:NVEC], vec_rows[0:NVEC - KT, 1, :],
                             ident[0:NVEC - KT, 0:NVEC - KT]).then_inc(vec_turned, 1)

            def gate_up(f, c, jobs, free=True, need=None):
                n = GU0[f] + c * 2 * ND
                for j, (k0, kn) in enumerate(HALVES_D):
                    if need and k0 in need:
                        pe.wait_ge(turned, need[k0])
                    half(n + j, j, k0, kn, xt_hi, xt_lo, gate_ps, KT - 1, gate_done,
                         (gate_taken, 2 * (CHUNKS * f + c - 1)) if free and j == 0 else None)
                    if j in jobs:
                        jobs[j]()
                for j, (k0, kn) in enumerate(HALVES_D):
                    half(n + ND + j, j, k0, kn, xt_hi, xt_lo, up_ps, KT - 1, up_done,
                         (gated_ready, 2 * (CHUNKS * f + c - 1)) if free and j == 0 else None)

            def turn_gated(f, c):
                turn_stage(TA[f] + 2 * c, gated_ready, 2 * (CHUNKS * f + c) + 2)

            def down(f, g, job, first=False):
                n = DN0[f] + g * NF
                for j, (k0, kn) in enumerate(HALVES_F):
                    if first and k0 + kn > FT - 4:
                        pe.wait_ge(turned, TA[f] + 2 * CHUNKS)
                    half(n + j, j, k0, kn, at_hi[f], at_lo[f], y_ps, FT - 1, y_done,
                         (x_ready, 2 * (2 * XG * f + g - 1)) if j == 0 and not first else None)
                    if j == 1:
                        job()

            def ffn(f):
                if f:
                    gate_up(f, 0, {1: lambda: turn_stage(TY2 + 2 * (XG - 1), x_ready, 4 * XG)}, free=False,
                            need={0: TY2 + 2 * (XG - 1), (XG - 1) * 4: TY2 + 2 * XG})
                else:
                    gate_up(f, 0, {1: lambda: turn_x(2), 3: lambda: turn_x(3), 4: turn_vectors}, free=False,
                            need={k: TX0 + k // 2 + 2 for k in range(0, KT, 4)})
                with pe.Fori(1, CHUNKS) as c:
                    gate_up(f, c, {1: lambda: turn_gated(f, c - 1)})
                down(f, 0, lambda: turn_gated(f, CHUNKS - 1), first=True)
                with pe.Fori(1, XG) as g:
                    down(f, g, (lambda: None) if f else
                         (lambda: turn_stage(TY1 + 2 * (g - 1), x_ready, 2 * (2 * XG * f + g - 1) + 2)))

            pe.wait_ge(ident_ready, 2)
            pe.wait_ge(vec_landed, 16)
            pe.transpose(y_ps[:, 0, 0:KT], vec_rows[0:KT, 0, :], ident[0:KT, 0:KT]).then_inc(vec_turned, 1)
            turn_x(0)
            turn_x(1)
            ffn(0)

            def turn_blocks(u, blocks):
                pe.wait_ge(turned, u - 1)
                for i, blk in enumerate(blocks):
                    mm = pe.transpose(turn_ps[:, u % 2, i * P:(i + 1) * P], blk, ident[:, :])
                mm.then_inc(turn_full, 1)

            def turn_rows(u, src, tiles):
                turn_blocks(u, [src[:, t, k * P:(k + 1) * P] for k in tiles for t in range(TOK)])

            def turn_ws():
                pe.wait_ge(ws_landed, 16)
                for b in range(2):
                    turn_blocks(TWS + b, [ws_raw[:, 4 * b + i, :] for i in range(4)])

            def turn_qk(g):
                pe.wait_ge(qk_scaled, g + 1)
                src = q_sb if g < 2 else k_sb
                for b in range(2):
                    h = 4 * (g % 2) + 2 * b
                    turn_rows(TQK + 2 * g + b, src, (h, h + 1))

            def scores(h):
                pe.wait_ge(turned, TQK + 8)
                if h:
                    pe.wait_ge(max_ready, h)
                pe.matmul(y_ps[:, 0, 0:P], qt[:, h, 0:P], kt[:, h, 0:P], start=True, stop=True)
                pe.matmul(y_ps[:, 0, P:3 * P], qt[:, h, P:2 * P], kt[:, h, :],
                          start=True, stop=True).then_inc(s_done, 1)

            def turn_p(h):
                pe.wait_ge(p_ready, 2 * h + 2)
                turn_blocks(TP + h, [s_sb[:, h % 2, i * P:(i + 1) * P] for i in range(3)])

            def values(h):
                pe.wait_ge(turned, TP + h + 1)
                if h:
                    pe.wait_ge(o_taken, h)
                pe.wait_ge(proj_taken, 2 * 6 if h >= 4 else 2 * 5)
                v = [v_sb[:, t, h * HD:(h + 1) * HD] for t in range(TOK)]
                pe.matmul(y_ps[:, 1, 0:P], pt[:, h % 2, 0:P], v[0], start=True, stop=True)
                pe.matmul(y_ps[:, 1, P:2 * P], pt[:, h % 2, P:2 * P], v[0], start=True, stop=False)
                pe.matmul(y_ps[:, 1, P:2 * P], pt[:, h % 2, 2 * P:3 * P], v[1],
                          start=False, stop=True).then_inc(o_done, 1)

            def turn_attn(i):
                pe.wait_ge(attn_scaled, 2)
                for b in range(2):
                    turn_rows(TAT + 2 * i + b, q_sb, (4 * i + 2 * b, 4 * i + 2 * b + 1))

            def spatial(i):
                pe.wait_ge(ws_masked, 1)
                pe.wait_ge(ln_ready, 2 * i + 2)
                pe.wait_ge(o_taken, HEADS)
                if i:
                    pe.wait_ge(mixed_taken, 2)
                for t in range(TOK):
                    for g in range(4 * i, 4 * i + 4):
                        mm = pe.matmul(y_ps[:, t, (g % 4) * P:(g % 4 + 1) * P], wst[:, g, :],
                                       k_sb[:, t, g * P:(g + 1) * P], start=True, stop=True)
                    mm.then_inc(mixed_done, 1)

            def turn_sgu(i):
                pe.wait_ge(sgu_scaled, 2)
                for b in range(2):
                    turn_rows(TSG + 2 * i + b, k_sb, (4 * i + 2 * b, 4 * i + 2 * b + 1))

            jobs = {1: [lambda: turn_stage(TY1 + 2 * (XG - 1), x_ready, 2 * XG)], 8: [turn_ws],
                    66: [lambda: turn_attn(0), lambda: spatial(0)], 67: [lambda: turn_attn(1)],
                    74: [lambda: spatial(1)], 82: [lambda: turn_sgu(0)], 83: [lambda: turn_sgu(1)]}
            for g in range(4):
                jobs.setdefault(12 + 8 * g, []).append(lambda g=g: turn_qk(g))
            for h in range(HEADS):
                jobs.setdefault(40 + 2 * h, []).append(lambda h=h: scores(h))
                jobs.setdefault(43 + 2 * h, []).append(lambda h=h: turn_p(h))
                jobs.setdefault(45 + 2 * h, []).append(lambda h=h: values(h))

            for m in range(PG * ND):
                g, j = m // ND, m % ND
                k0, kn = HALVES_D[j]
                if m == 0:
                    pe.wait_ge(turned, TY1 + 2 * (XG - 1))
                if m == 6:
                    pe.wait_ge(turned, TY1 + 2 * XG)
                half(IN0 + m, j, k0, kn, xt_hi, xt_lo, psum_of[g % 2], KT - 1, proj_done,
                     (proj_taken, 2 * (g - 2)) if g >= 2 and j == 0 else None)
                for job in jobs.get(m, []):
                    job()

            def out_group(g, job, first=False):
                for j, (k0, kn) in enumerate(HALVES_D):
                    if first and k0 in (0, KT // 2, KT // 2 + 4):
                        pe.wait_ge(turned, {0: TAT + 4, KT // 2: TSG + 2, KT // 2 + 4: TSG + 4}[k0])
                    if first and j == 0:
                        pe.wait_ge(mixed_taken, 4)
                    half(OUT0 + g * ND + j, j, k0, kn, mt_hi, mt_lo, y_ps, KT - 1, y_done,
                         (x_ready, 2 * (XG + g - 1)) if j == 0 and not first else None)
                    job(j)

            out_group(0, lambda j: [f() for f in jobs.get(PG * ND + j, [])], first=True)
            with pe.Fori(1, XG) as g:
                out_group(g, lambda j: turn_stage(TY2 + 2 * (g - 1), x_ready, 2 * (XG + g - 1) + 2)
                          if j == 1 else None)
            ffn(1)

        @block.scalar
        def _(act):
            def round_high(n, j, halves, uses, first=False):
                slot = (j // 2) % RAW
                kn, at = halves[j][1], (halves[j][0] - halves[j - j % 2][0]) * NCOL
                if j % 2 == 0:
                    act.wait_ge(raw_landed[slot], 16 * uses + 16)
                if not first:
                    act.wait_ge(split_used, n - SPL + 1)
                act.activation(w_hi[:, j % SPL, 0:kn * NCOL],
                               raw[:, slot, at:at + kn * NCOL],
                               ACT.Copy).then_inc(hi_ready, 1)

            def split_group(u0, g, row):
                for b in range(2):
                    act.wait_ge(turn_full, u0 + b + 1)
                    for kk in range(2):
                        k = 4 * g + 2 * b + kk
                        ins = act.activation(xt_hi[:, bass.ds(k, 1), :], turn_ps[:, b:b + 1, kk * 256:(kk + 1) * 256],
                                             ACT.Copy, scale=vec[:, bass.ds(row + k, 1)])
                    ins.then_inc(turn_high, 1)

            def split_gated(f, c):
                for b in range(2):
                    act.wait_ge(turn_full, TA[f] + 2 * c + b + 1)
                    act.activation(at_hi[f][:, bass.ds(4 * c + 2 * b, 2), :],
                                   turn_ps[:, b, :].rearrange("p (k t) -> p k t", k=2),
                                   ACT.Copy).then_inc(turn_high, 1)

            def silu(f, c):
                for t in range(TOK):
                    sum_done(act, gate_done, CHUNKS * f + c, GU0[f] + 2 * ND * c + ND - 1, t)
                    act.activation(stage[:, t, :], gate_ps[:, t, :], ACT.Silu,
                                   scale=root[:, ROOTS.index(["ffn1", "ffn2"][f]), t:t + 1]).then_inc(gate_taken, 1)

            def gate_up(f, c, jobs, first=False):
                n = GU0[f] + c * 2 * ND
                uses = GU0[f] // (2 * RAW) + c * 2
                for j in range(ND):
                    round_high(n + j, j, HALVES_D, uses, first and j < SPL)
                    if j in jobs:
                        jobs[j]()
                for j in range(ND):
                    round_high(n + ND + j, j, HALVES_D, uses + 1)
                    if j == 2:
                        silu(f, c)

            def down(f, g, job):
                for j in range(NF):
                    round_high(DN0[f] + g * NF + j, j, HALVES_F, DN0[f] // (2 * RAW) + g * 3 + j // (2 * RAW))
                    if j == 5:
                        job()

            def ffn(f):
                if f:
                    def job():
                        split_group(TY2 + 2 * (XG - 1), XG - 1, V_FFN2)
                        act.wait_ge(x_saved, 2 * XG)
                        act.wait_ge(root_ready, ROOTS.index("ffn2") + 1)
                    gate_up(1, 0, {5: job})
                else:
                    gate_up(0, 0, {1: lambda: split_group(TX0 + 2, 1, V_FFN1),
                                   3: lambda: split_group(TX0 + 4, 2, V_FFN1),
                                   5: lambda: split_group(TX0 + 6, 3, V_FFN1),
                                   7: lambda: (act.wait_ge(root_ready, 1), act.wait_ge(vec_ready, 2))}, first=True)
                with act.Fori(1, CHUNKS) as c:
                    gate_up(f, c, {5: lambda: split_gated(f, c - 1)})
                down(f, 0, lambda: split_gated(f, CHUNKS - 1))
                with act.Fori(1, XG) as g:
                    down(f, g, (lambda: None) if f else (lambda: split_group(TY1 + 2 * (g - 1), g - 1, V_MIX)))

            act.dma_start(vec_rows[0:KT, 0, :], ffn1_norm[0].rearrange("(k p) -> k p", p=P)).then_inc(vec_landed, 16)
            act.wait_ge(vec_ready, 1)
            split_group(TX0, 0, V_FFN1)
            ffn(0)

            root_mix = root[:, ROOTS.index("mix"), :]

            def take(g):
                dst = [q_sb, k_sb, v_sb, k_sb, None][g // 2]
                c = (g % 2) * NCOL
                if g == 9:
                    act.wait_ge(gated_u, 2)
                for t in range(TOK):
                    sum_done(act, proj_done, g, IN0 + ND * g + ND - 1, t)
                    to = stage[:, t, :] if dst is None else dst[:, t, c:c + NCOL]
                    act.activation(to, psum_of[g % 2][:, t, :], ACT.Gelu_apprx_tanh if g >= 6 else ACT.Copy,
                                   scale=root_mix[:, t:t + 1]).then_inc(proj_taken, 1)

            def exps(h):
                act.wait_ge(max_ready, h + 1)
                for t, (a, b) in enumerate(((0, P), (P, 3 * P))):
                    act.activation(s_sb[:, h % 2, a:b], s_sb[:, h % 2, a:b], ACT.Exp, bias=neg_max[:, h, t:t + 1],
                                   accum_out=row_sum[:, h, t:t + 1]).then_inc(p_ready, 1)

            def split_mixed(u, k, row):
                act.wait_ge(turn_full, u + 1)
                for kk in range(2):
                    ins = act.activation(mt_hi[:, k + kk, :], turn_ps[:, u % 2, kk * 256:(kk + 1) * 256],
                                         ACT.Copy, scale=vec[:, row + kk:row + kk + 1])
                ins.then_inc(turn_high, 1)

            def x_job():
                split_group(TY1 + 2 * (XG - 1), XG - 1, V_MIX)
                act.wait_ge(root_ready, ROOTS.index("mix") + 1)

            jobs = {5: [x_job]}
            for g, m in enumerate((10, 18, 26, 34, 42, 50, 59, 66, 74, 82)):
                jobs.setdefault(m, []).append(lambda g=g: take(g))
            for h in range(HEADS):
                jobs.setdefault(44 + 2 * h, []).append(lambda h=h: exps(h))
            for i in range(4):
                jobs.setdefault(69 + i // 2, []).append(lambda i=i: split_mixed(TAT + i, 2 * i, V_ATT + 2 * i))
                jobs.setdefault(85 + i // 2, []).append(
                    lambda i=i: split_mixed(TSG + i, KT // 2 + 2 * i, V_SGU + 2 * i))

            for m in range(PG * ND):
                g, j = m // ND, m % ND
                round_high(IN0 + m, j, HALVES_D, IN0 // (2 * RAW) + g)
                for job in jobs.get(m, []):
                    job()

            def out_group(g, job):
                for j in range(ND):
                    round_high(OUT0 + g * ND + j, j, HALVES_D, OUT0 // (2 * RAW) + g)
                    job(j)

            out_group(0, lambda j: [f() for f in jobs.get(PG * ND + j, [])])
            with act.Fori(1, XG) as g:
                out_group(g, lambda j: split_group(TY2 + 2 * (g - 1), g - 1, V_FFN2) if j == 5 else None)
            ffn(1)

        @block.vector
        def _(dve):
            steps = [0]

            def link(ins):
                steps[0] += 1
                ins.then_inc(dve_step, 1)
                dve.wait_ge(dve_step, steps[0])

            def rest_low(n, j, halves):
                slot = (j // 2) % RAW
                kn, at = halves[j][1], (halves[j][0] - halves[j - j % 2][0]) * NCOL
                dve.wait_ge(hi_ready, n + 1)
                dve.tensor_tensor(w_lo[:, j % SPL, 0:kn * NCOL],
                                  raw[:, slot, at:at + kn * NCOL],
                                  w_hi[:, j % SPL, 0:kn * NCOL].bitcast(F32), ALU.subtract).then_inc(lo_ready, 1)

            def split_group(s0, g, row):
                for b in range(2):
                    dve.wait_ge(turn_high, s0 + b + 1)
                    for kk in range(2):
                        k = 4 * g + 2 * b + kk
                        ins = dve.scalar_tensor_tensor(
                            out=xt_lo[:, bass.ds(k, 1), :], in0=turn_ps[:, b:b + 1, kk * 256:(kk + 1) * 256],
                            scalar=vec[:, bass.ds(row + k, 1)], in1=xt_hi[:, bass.ds(k, 1), :].bitcast(F32),
                            op0=ALU.mult, op1=ALU.subtract)
                    ins.then_inc(turned, 1)

            def split_gated(f, c):
                for b in range(2):
                    dve.wait_ge(turn_high, SA[f] + 2 * c + b + 1)
                    k = bass.ds(4 * c + 2 * b, 2)
                    dve.tensor_tensor(at_lo[f][:, k, :], turn_ps[:, b, :].rearrange("p (k t) -> p k t", k=2),
                                      at_hi[f][:, k, :].bitcast(F32), ALU.subtract).then_inc(turned, 1)

            def gated(f, c):
                for t in range(TOK):
                    dve.wait_ge(gate_taken, 2 * (CHUNKS * f + c) + t + 1)
                    sum_done(dve, up_done, CHUNKS * f + c, GU0[f] + 2 * ND * c + 2 * ND - 1, t)
                    dve.scalar_tensor_tensor(out=stage[:, t, :], in0=up_ps[:, t, :],
                                             scalar=root[:, ROOTS.index(["ffn1", "ffn2"][f]), t:t + 1],
                                             in1=stage[:, t, :], op0=ALU.mult, op1=ALU.mult).then_inc(gated_ready, 1)

            def add_x(y, g, scale, last_half, leaves=False):
                for t in range(TOK):
                    sum_done(dve, y_done, y, last_half, t)
                    if leaves:
                        dve.wait_ge(out_landed[t], 16 * g)
                    dve.scalar_tensor_tensor(out=stage[:, t, :], in0=y_ps[:, t, :], scalar=scale,
                                             in1=x_sb[:, t, bass.ts(g, NCOL)], op0=ALU.mult, op1=ALU.add)\
                       .then_inc(x_ready, 1)

            def keep_x(y, g):
                dve.wait_ge(x_ready, 2 * y + 2)
                for t in range(TOK):
                    dve.bn_stats(stats[:, t, g, :] if isinstance(g, int) else stats[:, t, bass.ds(g, 1), :],
                                 stage[:, t, :]).then_inc(dve_step, 1)
                dve.tensor_copy(x_sb[:, :, bass.ts(g, NCOL)], stage[:, :, :]).then_inc(x_saved, 1)

            def mean_square(name, src, n):
                i = ROOTS.index(name)
                for t in range(TOK):
                    link(dve.bn_aggr(agg[:, t, :], src[:, t, 0:n, :].rearrange("p a b -> p (a b)")))
                link(dve.tensor_tensor(mean_sq[:, i, 0:2], agg[:, :, 0], agg[:, :, 0], ALU.mult))
                dve.scalar_tensor_tensor(out=mean_sq[:, i, 0:2], in0=mean_sq[:, i, 0:2], scalar=EPS, in1=agg[:, :, 1],
                                         op0=ALU.add, op1=ALU.add).then_inc(ms_ready, 1)

            def gate_up(f, c, jobs):
                n = GU0[f] + c * 2 * ND
                for j in range(2 * ND):
                    rest_low(n + j, j % ND, HALVES_D)
                    if j in jobs:
                        jobs[j]()

            def down(f, g, jobs):
                for j in range(NF):
                    rest_low(DN0[f] + g * NF + j, j, HALVES_F)
                    if j in jobs:
                        jobs[j]()

            def ffn(f):
                y0 = 2 * XG * f
                if f:
                    def end_stats():
                        keep_x(2 * XG - 1, XG - 1)
                        steps[0] += 2
                        dve.wait_ge(dve_step, steps[0])
                        mean_square("ffn2", stats, XG)

                    gate_up(1, 0, {1: lambda: add_x(2 * XG - 1, XG - 1, 1.0, GU0[1] - 1), 3: end_stats, 5: lambda: split_group(SY2 + 2 * (XG - 1), XG - 1, V_FFN2),
                                   6: lambda: dve.wait_ge(root_ready, ROOTS.index("ffn2") + 1)})
                else:
                    def x_stats(g):
                        for t in range(TOK):
                            dve.bn_stats(stats[:, t, g, :], x_sb[:, t, g * NCOL:(g + 1) * NCOL]).then_inc(dve_step, 1)
                            steps[0] += 1

                    def split_and_stats(g):
                        split_group(SX0 + 2 * g, g, V_FFN1)
                        x_stats(g - 1)

                    def end_stats():
                        dve.wait_ge(x_landed[XG - 1], 16)
                        x_stats(XG - 1)
                        dve.wait_ge(dve_step, steps[0])
                        mean_square("ffn1", stats, XG)

                    def take_vectors():
                        dve.wait_ge(vec_turned, 2)
                        dve.tensor_copy(vec[:, KT:NVEC], y_ps[:, 0, KT:NVEC]).then_inc(vec_ready, 1)

                    gate_up(0, 0, {1: lambda: split_and_stats(1), 3: lambda: split_and_stats(2),
                                   5: lambda: split_and_stats(3), 6: end_stats, 7: take_vectors,
                                   9: lambda: dve.wait_ge(root_ready, 1)})
                with dve.Fori(1, CHUNKS) as c:
                    gate_up(f, c, {2: lambda: gated(f, c - 1), 5: lambda: split_gated(f, c - 1)})
                down(f, 0, {2: lambda: gated(f, CHUNKS - 1), 5: lambda: split_gated(f, CHUNKS - 1)})
                if f:
                    down(f, 1, {1: lambda: add_x(y0, 0, 0.5, DN0[f] + NF - 1)})
                    with dve.Fori(2, XG) as g:
                        down(f, g, {1: lambda: add_x(y0 + g - 1, g - 1, 0.5, DN0[f] + NF * g - 1, leaves=True)})
                    add_x(y0 + XG - 1, XG - 1, 0.5, DN0[f] + NF * XG - 1, leaves=True)
                else:
                    with dve.Fori(1, XG) as g:
                        down(f, g, {1: lambda: add_x(g - 1, g - 1, 0.5, DN0[f] + NF * g - 1),
                                    3: lambda: keep_x(g - 1, g - 1), 5: lambda: split_group(SY1 + 2 * (g - 1), g - 1, V_MIX)})
                    steps[0] += 2 * (XG - 1)

            dve.memset(neg_half[:, :], -0.5).then_inc(ident_ready, 1)
            dve.wait_ge(vec_turned, 1)
            dve.tensor_copy(vec[:, 0:KT], y_ps[:, 0, 0:KT]).then_inc(vec_ready, 1)
            dve.wait_ge(vec_ready, 1)
            split_group(SX0, 0, V_FFN1)
            ffn(0)

            def copy_ws():
                for b in range(2):
                    dve.wait_ge(turn_full, TWS + b + 1)
                    dve.tensor_copy(wst[:, 4 * b:4 * b + 4, :],
                                    turn_ps[:, b, :].rearrange("p (g t) -> p g t", t=P)).then_inc(turned, 1)

            def end_x():
                keep_x(XG - 1, XG - 1)
                steps[0] += 2
                dve.wait_ge(dve_step, steps[0])
                mean_square("mix", stats, XG)

            def qk_squares(g):
                src = q_sb if g < 2 else k_sb
                c = (g % 2) * NCOL
                if g == 0:
                    dve.wait_ge(x_saved, XG)
                for t in range(TOK):
                    dve.wait_ge(proj_taken, 2 * g + t + 1)
                    link(dve.tensor_tensor(stage[:, t, :], src[:, t, c:c + NCOL], src[:, t, c:c + NCOL], ALU.mult))
                    link(dve.tensor_reduce(sq_sum[:, t, :], stage[:, t, :].rearrange("p (h d) -> p h d", d=HD),
                                           AXX, ALU.add))
                dve.tensor_scalar(mean_sq[:, ROOTS.index(f"qk{g}"), :], sq_sum[:, :, :].rearrange("p t h -> p (t h)"),
                                  1.0 / HD, EPS, ALU.mult, ALU.add).then_inc(ms_ready, 1)

            def qk_scale(g):
                src = q_sb if g < 2 else k_sb
                c = (g % 2) * NCOL
                i = ROOTS.index(f"qk{g}")
                dve.wait_ge(root_ready, i + 1)
                for t in range(TOK):
                    v = src[:, t, c:c + NCOL].rearrange("p (h d) -> p h d", d=HD)
                    ins = dve.tensor_tensor(v, v, root[:, i, 4 * t:4 * t + 4, None].to_broadcast([P, 4, HD]), ALU.mult)
                ins.then_inc(qk_scaled, 1)

            def qk_turned(g):
                dst, col = (qt, V_Q) if g < 2 else (kt, V_K)
                for b in range(2):
                    h = 4 * (g % 2) + 2 * b
                    dve.wait_ge(turn_full, TQK + 2 * g + b + 1)
                    dve.tensor_scalar(dst[:, h:h + 2, :], turn_ps[:, b, :].rearrange("p (h t) -> p h t", h=2),
                                      vec[:, col:col + 1], None, ALU.mult).then_inc(turned, 1)

            def masked_max(h):
                dve.wait_ge(s_done, h + 1)
                if h == 0:
                    dve.wait_ge(mask_ready, 1)
                if h >= 2:
                    dve.wait_ge(turn_full, TP + h - 1)
                link(dve.scalar_tensor_tensor(out=s_sb[:, h % 2, :], in0=y_ps[:, 0, 0:3 * P], scalar=SCALE,
                                              in1=mask[:, :], op0=ALU.mult, op1=ALU.add))
                dve.tensor_reduce(neg_max[:, h, 0:1], s_sb[:, h % 2, 0:P], AXX, ALU.max, negate=True)
                dve.tensor_reduce(neg_max[:, h, 1:2], s_sb[:, h % 2, P:3 * P], AXX, ALU.max,
                                  negate=True).then_inc(max_ready, 1)

            def take_p(h):
                dve.wait_ge(p_ready, 2 * h + 2)
                dve.wait_ge(turn_full, TP + h + 1)
                if h >= 2:
                    dve.wait_ge(o_done, h - 1)
                dve.tensor_copy(pt[:, h % 2, :], turn_ps[:, (TP + h) % 2, 0:3 * P]).then_inc(turned, 1)
                link(dve.reciprocal(inv_sum[:, h, :], row_sum[:, h, :]))

            def take_o(h):
                dve.wait_ge(o_done, h + 1)
                for t in range(TOK):
                    ins = dve.tensor_scalar(q_sb[:, t, h * HD:(h + 1) * HD], y_ps[:, 1, t * P:(t + 1) * P],
                                            inv_sum[:, h, t:t + 1], None, ALU.mult)
                ins.then_inc(o_taken, 1)

            def row_stats(src, c):
                for t in range(TOK):
                    ins = dve.bn_stats(stats[:, t, c, :], src[:, t, c * NCOL:(c + 1) * NCOL])
                link(ins)

            def attn_square():
                dve.wait_ge(o_taken, HEADS)
                row_stats(q_sb, 0)
                row_stats(q_sb, 1)
                mean_square("attn", stats, 2)

            def scale_rows(name, src, done):
                i = ROOTS.index(name)
                dve.wait_ge(root_ready, i + 1)
                for t in range(TOK):
                    dve.tensor_scalar(src[:, t, :], src[:, t, :], root[:, i, t:t + 1], None, ALU.mult).then_inc(done, 1)

            def split_mixed(u, s, k, row):
                dve.wait_ge(turn_high, s + 1)
                for kk in range(2):
                    ins = dve.scalar_tensor_tensor(
                        out=mt_lo[:, k + kk, :], in0=turn_ps[:, u % 2, kk * 256:(kk + 1) * 256],
                        scalar=vec[:, row + kk:row + kk + 1], in1=mt_hi[:, k + kk, :].bitcast(F32),
                        op0=ALU.mult, op1=ALU.subtract)
                ins.then_inc(turned, 1)

            def ln_square(i):
                for t in range(TOK):
                    dve.wait_ge(proj_taken, 2 * (6 + i) + t + 1)
                    for g in range(4):
                        ins = dve.bn_stats(ln_stats[:, t, g, :], k_sb[:, t, (4 * i + g) * P:(4 * i + g + 1) * P])
                link(ins)
                for t in range(TOK):
                    for g in range(4):
                        ins = dve.bn_aggr(ln_agg[:, t, g, :], ln_stats[:, t, g, :])
                link(ins)
                dve.tensor_scalar(mean_sq[:, ROOTS.index(f"ln{i}"), :].rearrange("p (t g) -> p t g", t=2),
                                  ln_agg[:, :, :, 1], EPS, None, ALU.add).then_inc(ms_ready, 1)

            def ln_scale(i, t):
                r = ROOTS.index(f"ln{i}")
                dve.wait_ge(root_ready, r + 1)
                dve.wait_ge(ln_landed, 32)
                for g in range(4):
                    v = k_sb[:, t, (4 * i + g) * P:(4 * i + g + 1) * P]
                    ins = dve.tensor_scalar(v, v, ln_agg[:, t, g, 0:1], root[:, r, 4 * t + g:4 * t + g + 1],
                                            ALU.subtract, ALU.mult)
                link(ins)
                v = k_sb[:, t, i * NCOL:(i + 1) * NCOL]
                link(dve.tensor_tensor(v, v, ln_rows[:, 0, i * NCOL:(i + 1) * NCOL], ALU.mult))
                dve.tensor_tensor(v, v, ln_rows[:, 1, i * NCOL:(i + 1) * NCOL], ALU.add).then_inc(ln_ready, 1)

            def take_mixed(i):
                for t in range(TOK):
                    dve.wait_ge(mixed_done, 2 * i + 2)
                    dve.tensor_tensor(k_sb[:, t, i * NCOL:(i + 1) * NCOL].rearrange("p (g c) -> p g c", c=P),
                                      y_ps[:, t, :].rearrange("p (g c) -> p g c", c=P),
                                      vec[:, V_BS + 4 * i:V_BS + 4 * i + 4, None].to_broadcast([P, 4, P]),
                                      ALU.add).then_inc(mixed_taken, 1)

            def gate_u(i):
                for t in range(TOK):
                    dve.wait_ge(proj_taken, 2 * (8 + i) + t + 1)
                    dve.wait_ge(mixed_taken, 2 * i + t + 1)
                    v = k_sb[:, t, i * NCOL:(i + 1) * NCOL]
                    dve.tensor_tensor(v, v, stage[:, t, :], ALU.mult).then_inc(gated_u, 1)

            def sgu_stats(i):
                dve.wait_ge(gated_u, 2 * i + 2)
                row_stats(k_sb, i)

            jobs = {1: [lambda: add_x(XG - 1, XG - 1, 0.5, IN0 - 1)], 3: [end_x], 5: [lambda: split_group(SY1 + 2 * (XG - 1), XG - 1, V_MIX)], 11: [copy_ws],
                    61: [lambda: ln_square(0)], 62: [lambda: ln_scale(0, 0)], 63: [lambda: ln_scale(0, 1)],
                    64: [attn_square], 65: [lambda: scale_rows("attn", q_sb, attn_scaled)],
                    67: [lambda: ln_square(1)], 71: [lambda: ln_scale(1, 0)], 72: [lambda: ln_scale(1, 1)],
                    68: [lambda: take_mixed(0)], 76: [lambda: gate_u(0)], 77: [lambda: take_mixed(1)],
                    78: [lambda: sgu_stats(0)],
                    82: [lambda: gate_u(1), lambda: sgu_stats(1), lambda: mean_square("sgu", stats, 2),
                         lambda: scale_rows("sgu", k_sb, sgu_scaled)]}
            for g in range(4):
                jobs.setdefault(11 + 8 * g, []).append(lambda g=g: qk_squares(g))
                jobs.setdefault(13 + 8 * g, []).append(lambda g=g: qk_scale(g))
                jobs.setdefault(15 + 8 * g, []).append(lambda g=g: qk_turned(g))
            for h in range(HEADS):
                jobs.setdefault(43 + 2 * h, []).append(lambda h=h: masked_max(h))
                jobs.setdefault(46 + 2 * h, []).append(lambda h=h: take_p(h))
                jobs.setdefault(48 + 2 * h, []).append(lambda h=h: take_o(h))
            for i in range(4):
                jobs.setdefault(69 + i // 2, []).append(
                    lambda i=i: split_mixed(TAT + i, SAT + i, 2 * i, V_ATT + 2 * i))
                jobs.setdefault(85 + i // 2, []).append(
                    lambda i=i: split_mixed(TSG + i, SSG + i, KT // 2 + 2 * i, V_SGU + 2 * i))

            for m in range(PG * ND):
                rest_low(IN0 + m, m % ND, HALVES_D)
                for job in jobs.get(m, []):
                    job()

            def out_group(g, jobs_of):
                for j in range(ND):
                    rest_low(OUT0 + g * ND + j, j, HALVES_D)
                    for job in jobs_of.get(j, []):
                        job()

            out_group(0, {j: jobs.get(PG * ND + j, []) for j in range(ND)})
            with dve.Fori(1, XG) as g:
                out_group(g, {1: [lambda: add_x(XG + g - 1, g - 1, 1.0, OUT0 + ND * g - 1)],
                              3: [lambda: keep_x(XG + g - 1, g - 1)], 5: [lambda: split_group(SY2 + 2 * (g - 1), g - 1, V_FFN2)]})
            steps[0] += 2 * (XG - 1)
            ffn(1)

        @block.gpsimd
        def _(pool):
            pool.memset(ident[:, :], 0.0).then_inc(pool_step, 1)
            pool.wait_ge(pool_step, 1)
            pool.affine_select(out=ident[:, :], in_=ident[:, :], compare_op=ALU.not_equal, fill=1.0, base=0,
                               pattern=[[-1, P]], channel_multiplier=1).then_inc(ident_ready, 1)

            r = 0
            for src in (mix_norm, ffn2_norm, attn_out_gain, sgu_out_gain, q_norm, k_norm):
                rows = src[0].rearrange("(k p) -> k p", p=P)
                pool.dma_start(vec_rows[r:r + rows.shape[0], 1, :], rows).then_inc(vecs_landed, 16)
                r += rows.shape[0]
            pool.dma_start(vec_rows[r:r + SGU_G, 1, :], sgu_b_spatial[0]).then_inc(vecs_landed, 16)

            def roots(name, n=2):
                i = ROOTS.index(name)
                pool.wait_ge(ms_ready, i + 1)
                pool.tensor_tensor(root[:, i, 0:n], mean_sq[:, i, 0:n], neg_half[:, 0:n], ALU.pow)\
                    .then_inc(root_ready, 1)

            pool.wait_ge(ident_ready, 2)
            roots("ffn1")
            roots("mix")

            pool.wait_ge(split_used, IN0)
            pool.dma_start(ws_raw, sgu_w_spatial[0].rearrange("g t s -> t g s")).then_inc(ws_landed, 16)
            pool.memset(mask[:, :], 0.0).then_inc(pool_step, 1)
            pool.wait_ge(pool_step, 2)
            for n, a in enumerate((0, 2 * P)):
                pool.affine_select(out=mask[:, a:a + P], in_=mask[:, a:a + P], compare_op=ALU.is_ge, fill=NEG,
                                   base=0, pattern=[[-1, P]], channel_multiplier=1).then_inc(pool_step, 1)
            pool.wait_ge(pool_step, 4)
            pool.sem_inc(mask_ready, 1)
            roots("qk0", 8)
            pool.wait_ge(turned, TWS + 2)
            pool.affine_select(out=wst[:, :, :], in_=wst[:, :, :], compare_op=ALU.is_ge, fill=0.0, base=0,
                               pattern=[[0, SGU_G], [1, P]], channel_multiplier=-1).then_inc(ws_masked, 1)
            for g in range(1, 4):
                roots(f"qk{g}", 8)
            pool.wait_ge(s_done, HEADS)
            for i, v in enumerate((sgu_ln_gain, sgu_ln_bias)):
                pool.dma_start(ln_rows[:, i, :], v[0].rearrange("(a n) -> a n", a=1).to_broadcast([P, DATT]))\
                    .then_inc(ln_landed, 16)
            roots("ln0", 8)
            roots("attn")
            roots("ln1", 8)
            roots("sgu")
            roots("ffn2")
            with pool.Fori(0, XG - 1) as g:
                for t in range(TOK):
                    pool.wait_ge(x_ready, 4 * XG + 2 * g + t + 1)
                    pool.dma_start(out_rows[:, t, bass.ts(g, NCOL)], stage[:, t, :]).then_inc(out_landed[t], 16)
            for t in range(TOK):
                pool.wait_ge(out_landed[t], 16 * (XG - 1))


_INS = ["x", "ffn1_norm", "ffn1_w_gate", "ffn1_w_up", "ffn1_w_down", "mix_norm", "w_in", "q_norm", "k_norm",
        "sgu_ln_gain", "sgu_ln_bias", "sgu_w_spatial", "sgu_b_spatial", "attn_out_gain", "sgu_out_gain", "w_out",
        "ffn2_norm", "ffn2_w_gate", "ffn2_w_up", "ffn2_w_down"]


def kernel(**inputs):
    import numpy as np
    import concourse.bacc as bacc
    from concourse import mybir as mb
    from concourse.bass_utils import run_bass_kernel_spmd

    nc = bacc.Bacc("TRN2", target_bir_lowering=False, num_devices=1)
    arrays, args = {}, []
    for name in _INS:
        a = np.ascontiguousarray(inputs[name])
        arrays[f"in_{name}"] = a
        args.append(nc.dram_tensor(f"in_{name}", a.shape, mb.dt.from_np(a.dtype), kind="ExternalInput").ap())
    shape = tuple(inputs["x"].shape)
    args.append(nc.dram_tensor("out_x", shape, mb.dt.float32, kind="ExternalOutput").ap())
    build(nc, *args)
    r = run_bass_kernel_spmd(nc, [arrays], core_ids=[0])
    return r.results[0]["out_x"]
```
